# Optimizing a Trainium2 kernel written in Bass

```python
import jax, jax.numpy as jnp
from jax import lax
import numpy as np
import math

D_MODEL = 1024
BATCH = 1
SEQ = 512
DEPTH = 2

N_EVEN = (DEPTH + 1) // 2
N_ODD = DEPTH // 2

NSA_HEADS = 8
HEAD_DIM = 64
KV_GROUPS = 2
HEADS_PER_GROUP = NSA_HEADS // KV_GROUPS
N_BRANCH = 3
CMP_BLOCK = 32
CMP_STRIDE = 16
CMP_HIDDEN = 128
SEL_BLOCK = 64
SEL_TOPK = 8
WINDOW = 512
Q_BLOCK = 128
FORCE_BONUS = 1e4
NEG = -1e30

POOL_WIDTH = D_MODEL // 2
POOL_WINDOWS = (2, 4, 8, 16)
POOL_GROUPS = len(POOL_WINDOWS)
POOL_GROUP_DIM = POOL_WIDTH // POOL_GROUPS

NSA_WIDTH = NSA_HEADS * HEAD_DIM
KV_WIDTH = KV_GROUPS * HEAD_DIM
GATE_WIDTH = NSA_HEADS * N_BRANCH
IN_WIDTH = NSA_WIDTH + N_BRANCH * 2 * KV_WIDTH + GATE_WIDTH + POOL_WIDTH
MIX_WIDTH = NSA_WIDTH + POOL_WIDTH

CONV_WIDTH = 31

FFN_HIDDEN = -(-8 * D_MODEL // (3 * 256)) * 256


def rmsnorm(x, g, eps=1e-6):
    xf = x.astype(jnp.float32)
    y = xf * lax.rsqrt(jnp.mean(xf * xf, axis=-1, keepdims=True) + eps)
    return (y * g.astype(jnp.float32)).astype(x.dtype)

def layernorm(x, g, b, eps=1e-5):
    xf = x.astype(jnp.float32)
    mu = jnp.mean(xf, axis=-1, keepdims=True)
    xc = xf - mu
    var = jnp.mean(xc * xc, axis=-1, keepdims=True)
    y = xc * lax.rsqrt(var + eps) * g.astype(jnp.float32) + b.astype(jnp.float32)
    return y.astype(x.dtype)

def alibi_slopes():
    h = jnp.arange(1, NSA_HEADS + 1, dtype=jnp.float32)
    return jnp.exp2(-8.0 * h / NSA_HEADS).reshape(KV_GROUPS, HEADS_PER_GROUP)

def compress_blocks(kv, pos, w1, w2):
    b, g, s, dh = kv.shape
    r = CMP_BLOCK // CMP_STRIDE
    n_cmp = s // CMP_STRIDE - r + 1
    sub = kv.reshape(b, g, s // CMP_STRIDE, CMP_STRIDE, dh)
    blocks = jnp.concatenate([sub[:, :, j:j + n_cmp] for j in range(r)], axis=3)
    blocks = (blocks + pos).reshape(b, g, n_cmp, CMP_BLOCK * dh)
    return jax.nn.gelu(blocks @ w1) @ w2

def compressed_branch(q, kc, vc, slopes):
    s = q.shape[3]
    n_cmp = kc.shape[2]
    t = jnp.arange(s, dtype=jnp.int32)[:, None]
    end = jnp.arange(n_cmp, dtype=jnp.int32)[None, :] * CMP_STRIDE + (CMP_BLOCK - 1)
    dist = (t - end).astype(jnp.float32)
    valid = dist >= 0
    logits = jnp.einsum('bgrtd,bgnd->bgrtn', q, kc).astype(jnp.float32)
    logits = logits - slopes[:, :, None, None] * dist
    logits = jnp.where(valid, logits, NEG)
    p = jax.nn.softmax(logits, axis=-1) * valid
    o = jnp.einsum('bgrtn,bgnd->bgrtd', p.astype(vc.dtype), vc)
    return o, p

def selection_indices(p_cmp, s):
    n_cmp = p_cmp.shape[-1]
    n_sel = s // SEL_BLOCK
    c0 = np.arange(n_cmp)[:, None] * CMP_STRIDE
    s0 = np.arange(n_sel)[None, :] * SEL_BLOCK
    overlap = np.clip(np.minimum(c0 + CMP_BLOCK, s0 + SEL_BLOCK) - np.maximum(c0, s0), 0, None) / CMP_BLOCK
    imp = jnp.einsum('bgtn,nj->bgtj', p_cmp.sum(axis=2), jnp.asarray(overlap, jnp.float32))
    t_blk = (jnp.arange(s, dtype=jnp.int32) // SEL_BLOCK)[:, None]
    j = jnp.arange(n_sel, dtype=jnp.int32)[None, :]
    forced = (j == 0) | (j == t_blk) | (j == t_blk - 1)
    imp = jnp.where(forced, imp + FORCE_BONUS, imp)
    imp = jnp.where(j > t_blk, NEG, imp)
    _, idx = lax.top_k(imp, min(SEL_TOPK, n_sel))
    return idx

def selected_branch(q, ks, vs, idx, slopes):
    b, g, r, s, dh = q.shape
    k = idx.shape[-1]
    n_sel = s // SEL_BLOCK
    nq = s // Q_BLOCK
    kb = ks.reshape(b, g, n_sel, SEL_BLOCK, dh)
    vb = vs.reshape(b, g, n_sel, SEL_BLOCK, dh)
    qc = jnp.moveaxis(q.reshape(b, g, r, nq, Q_BLOCK, dh), 3, 0)
    ic = jnp.moveaxis(idx.reshape(b, g, nq, Q_BLOCK, k), 2, 0)
    tc = jnp.arange(s, dtype=jnp.int32).reshape(nq, Q_BLOCK)
    bi = jnp.arange(b)[:, None, None, None]
    gi = jnp.arange(g)[None, :, None, None]
    offs = jnp.arange(SEL_BLOCK, dtype=jnp.int32)

    def one_block(args):
        qq, ii, tt = args
        k_sel = kb[bi, gi, ii].reshape(b, g, Q_BLOCK, k * SEL_BLOCK, dh)
        v_sel = vb[bi, gi, ii].reshape(b, g, Q_BLOCK, k * SEL_BLOCK, dh)
        pos = (ii[..., None] * SEL_BLOCK + offs).reshape(b, g, Q_BLOCK, k * SEL_BLOCK)
        dist = (tt[None, None, :, None] - pos).astype(jnp.float32)[:, :, None]
        logits = jnp.einsum('bgrqd,bgqkd->bgrqk', qq, k_sel).astype(jnp.float32)
        logits = logits - slopes[None, :, :, None, None] * dist
        logits = jnp.where(dist >= 0, logits, NEG)
        p = jax.nn.softmax(logits, axis=-1)
        return jnp.einsum('bgrqk,bgqkd->bgrqd', p.astype(v_sel.dtype), v_sel)

    o = lax.map(one_block, (qc, ic, tc))
    return jnp.moveaxis(o, 0, 3).reshape(b, g, r, s, dh)

def window_branch(q, kw, vw, slopes):
    b, g, r, s, dh = q.shape
    nq = s // Q_BLOCK
    nw = WINDOW // Q_BLOCK
    pad = ((0, 0), (0, 0), (WINDOW, 0), (0, 0))
    kp = jnp.pad(kw, pad).reshape(b, g, nq + nw, Q_BLOCK, dh)
    vp = jnp.pad(vw, pad).reshape(b, g, nq + nw, Q_BLOCK, dh)
    k_band = jnp.concatenate([kp[:, :, j:j + nq] for j in range(nw + 1)], axis=3)
    v_band = jnp.concatenate([vp[:, :, j:j + nq] for j in range(nw + 1)], axis=3)
    qb = q.reshape(b, g, r, nq, Q_BLOCK, dh)
    t = jnp.arange(s, dtype=jnp.int32).reshape(nq, Q_BLOCK)
    kpos = (jnp.arange(nq, dtype=jnp.int32)[:, None] - nw) * Q_BLOCK + jnp.arange((nw + 1) * Q_BLOCK, dtype=jnp.int32)[None, :]
    dist = t[:, :, None] - kpos[:, None, :]
    valid = (dist >= 0) & (dist < WINDOW) & (kpos[:, None, :] >= 0)
    logits = jnp.einsum('bgrnqd,bgnkd->bgrnqk', qb, k_band).astype(jnp.float32)
    logits = logits - slopes[:, :, None, None, None] * dist.astype(jnp.float32)
    logits = jnp.where(valid, logits, NEG)
    p = jax.nn.softmax(logits, axis=-1)
    o = jnp.einsum('bgrnqk,bgnkd->bgrnqd', p.astype(v_band.dtype), v_band)
    return o.reshape(b, g, r, s, dh)

def multiscale_pool(u, w_pool, scale):
    b, s, c = u.shape
    uf = u.astype(jnp.float32)
    cs = jnp.pad(jnp.cumsum(uf, axis=1), ((0, 0), (1, 0), (0, 0)))
    t = jnp.arange(s, dtype=jnp.float32)
    outs = []
    for gi, w in enumerate(POOL_WINDOWS):
        sl = slice(gi * POOL_GROUP_DIM, (gi + 1) * POOL_GROUP_DIM)
        csg = cs[:, :, sl]
        start = jnp.pad(csg, ((0, 0), (w - 1, 0), (0, 0)))[:, :s]
        mean = (csg[:, 1:] - start) / jnp.minimum(t + 1.0, float(w))[None, :, None]
        outs.append(mean - uf[:, :, sl])
    d = jnp.stack(outs, axis=2).astype(u.dtype)
    y = jnp.einsum('bsgc,gce->bsge', d, w_pool).reshape(b, s, c)
    return y * scale

def nsa_pool_mixer(h, w_in, pos_k, pos_v, k_w1, k_w2, v_w1, v_w2, w_pool, pool_scale, w_out):
    b, s, _ = h.shape
    proj = h @ w_in
    sizes = [NSA_WIDTH] + [KV_WIDTH] * (2 * N_BRANCH) + [GATE_WIDTH]
    cuts = [int(c) for c in np.cumsum(sizes)]
    q, kc, vc, ks, vs, kw, vw, gate, u = jnp.split(proj, cuts, axis=-1)

    def kv_heads(z):
        return z.reshape(b, s, KV_GROUPS, HEAD_DIM).transpose(0, 2, 1, 3)

    q = q.reshape(b, s, KV_GROUPS, HEADS_PER_GROUP, HEAD_DIM).transpose(0, 2, 3, 1, 4) * (HEAD_DIM ** -0.5)
    slopes = alibi_slopes()

    kcmp = compress_blocks(kv_heads(kc), pos_k, k_w1, k_w2)
    vcmp = compress_blocks(kv_heads(vc), pos_v, v_w1, v_w2)
    o_cmp, p_cmp = compressed_branch(q, kcmp, vcmp, slopes)
    idx = selection_indices(p_cmp, s)
    o_sel = selected_branch(q, kv_heads(ks), kv_heads(vs), idx, slopes)
    o_win = window_branch(q, kv_heads(kw), kv_heads(vw), slopes)

    g = jax.nn.sigmoid(gate.reshape(b, s, KV_GROUPS, HEADS_PER_GROUP, N_BRANCH)).transpose(0, 2, 3, 1, 4)
    o = g[..., 0:1] * o_cmp + g[..., 1:2] * o_sel + g[..., 2:3] * o_win
    o = o.transpose(0, 3, 1, 2, 4).reshape(b, s, NSA_WIDTH)
    y_pool = multiscale_pool(u, w_pool, pool_scale)
    return jnp.concatenate([o, y_pool], axis=-1) @ w_out

def conformer_conv(h, w_pw1, b_pw1, w_dw, b_dw, ln_g, ln_b, w_pw2, b_pw2):
    a, gt = jnp.split(h @ w_pw1 + b_pw1, 2, axis=-1)
    z = a * jax.nn.sigmoid(gt)
    z = lax.conv_general_dilated(
        z, w_dw[:, None, :], window_strides=(1,), padding=[(CONV_WIDTH - 1, 0)],
        dimension_numbers=('NWC', 'WIO', 'NWC'), feature_group_count=D_MODEL) + b_dw
    z = jax.nn.silu(layernorm(z, ln_g, ln_b))
    return z @ w_pw2 + b_pw2

def swiglu(h, w_gate, w_up, w_down):
    return (jax.nn.silu(h @ w_gate) * (h @ w_up)) @ w_down

def first_inputs(seed: int = 0) -> dict:
    key = jax.random.key(seed)
    keys = iter(jax.random.split(key, 32))

    def nrm(shape, scale):
        return jax.random.normal(next(keys), shape, jnp.float32) * scale

    def gain(shape):
        return 1.0 + nrm(shape, 0.05)

    dh = HEAD_DIM
    return {
        "x": nrm((BATCH, SEQ, D_MODEL), 1.0),
        "mix_norm": gain((DEPTH, D_MODEL)),
        "ffn_norm": gain((DEPTH, D_MODEL)),
        "nsa_w_in": nrm((N_EVEN, D_MODEL, IN_WIDTH), D_MODEL ** -0.5),
        "cmp_pos_k": nrm((N_EVEN, CMP_BLOCK, dh), 0.1),
        "cmp_pos_v": nrm((N_EVEN, CMP_BLOCK, dh), 0.1),
        "cmp_k_w1": nrm((N_EVEN, CMP_BLOCK * dh, CMP_HIDDEN), (CMP_BLOCK * dh) ** -0.5),
        "cmp_k_w2": nrm((N_EVEN, CMP_HIDDEN, dh), CMP_HIDDEN ** -0.5),
        "cmp_v_w1": nrm((N_EVEN, CMP_BLOCK * dh, CMP_HIDDEN), (CMP_BLOCK * dh) ** -0.5),
        "cmp_v_w2": nrm((N_EVEN, CMP_HIDDEN, dh), CMP_HIDDEN ** -0.5),
        "pool_w": nrm((N_EVEN, POOL_GROUPS, POOL_GROUP_DIM, POOL_GROUP_DIM), POOL_GROUP_DIM ** -0.5),
        "pool_scale": gain((N_EVEN, POOL_WIDTH)),
        "mix_w_out": nrm((N_EVEN, MIX_WIDTH, D_MODEL), MIX_WIDTH ** -0.5),
        "conv_w_pw1": nrm((N_ODD, D_MODEL, 2 * D_MODEL), D_MODEL ** -0.5),
        "conv_b_pw1": nrm((N_ODD, 2 * D_MODEL), 0.02),
        "conv_w_dw": nrm((N_ODD, CONV_WIDTH, D_MODEL), CONV_WIDTH ** -0.5),
        "conv_b_dw": nrm((N_ODD, D_MODEL), 0.02),
        "conv_ln_g": gain((N_ODD, D_MODEL)),
        "conv_ln_b": nrm((N_ODD, D_MODEL), 0.02),
        "conv_w_pw2": nrm((N_ODD, D_MODEL, D_MODEL), D_MODEL ** -0.5),
        "conv_b_pw2": nrm((N_ODD, D_MODEL), 0.02),
        "ffn_w_gate": nrm((DEPTH, D_MODEL, FFN_HIDDEN), D_MODEL ** -0.5),
        "ffn_w_up": nrm((DEPTH, D_MODEL, FFN_HIDDEN), D_MODEL ** -0.5),
        "ffn_w_down": nrm((DEPTH, FFN_HIDDEN, D_MODEL), FFN_HIDDEN ** -0.5),
        "final_norm": gain((D_MODEL,)),
    }

def first_block(x, mix_norm, ffn_norm, nsa_w_in, cmp_pos_k, cmp_pos_v, cmp_k_w1, cmp_k_w2,
              cmp_v_w1, cmp_v_w2, pool_w, pool_scale, mix_w_out, conv_w_pw1, conv_b_pw1,
              conv_w_dw, conv_b_dw, conv_ln_g, conv_ln_b, conv_w_pw2, conv_b_pw2,
              ffn_w_gate, ffn_w_up, ffn_w_down, final_norm):
    for layer in range(DEPTH):
        h = rmsnorm(x, mix_norm[layer])
        i = layer // 2
        if layer % 2 == 0:
            x = x + nsa_pool_mixer(h, nsa_w_in[i], cmp_pos_k[i], cmp_pos_v[i], cmp_k_w1[i], cmp_k_w2[i],
                                   cmp_v_w1[i], cmp_v_w2[i], pool_w[i], pool_scale[i], mix_w_out[i])
        else:
            x = x + conformer_conv(h, conv_w_pw1[i], conv_b_pw1[i], conv_w_dw[i], conv_b_dw[i],
                                   conv_ln_g[i], conv_ln_b[i], conv_w_pw2[i], conv_b_pw2[i])
        h = rmsnorm(x, ffn_norm[layer])
        x = x + swiglu(h, ffn_w_gate[layer], ffn_w_up[layer], ffn_w_down[layer])
    return rmsnorm(x, final_norm)


DEPTH_2 = 1

GLA_HEADS = 4
GLA_DK = 64
GLA_DV = 128
GLA_QK_DIM = GLA_HEADS * GLA_DK
GLA_V_DIM = GLA_HEADS * GLA_DV
GATE_RANK = 16
GATE_NORMALIZER = 16.0
CHUNK = 64
CONV_DIM = 512
CONV_WIDTH_2 = 3
IN_SPLITS = (GLA_QK_DIM, GLA_QK_DIM, GLA_V_DIM, GLA_V_DIM, GATE_RANK, CONV_DIM, CONV_DIM, CONV_DIM)
IN_DIM = sum(IN_SPLITS)
MIX_DIM = GLA_V_DIM + CONV_DIM
FFN_HIDDEN_2 = int(math.ceil(8 * D_MODEL / 3 / 256) * 256)
PLE_DIM = 256
NORM_EPS = 1e-6


def _rmsnorm(x, g):
    xf = x.astype(jnp.float32)
    xf = xf * lax.rsqrt(jnp.mean(xf * xf, axis=-1, keepdims=True) + NORM_EPS)
    return (xf * g.astype(jnp.float32)).astype(x.dtype)

def _gla_chunked(q, k, v, log_a):
    b_, s_, h_, dk = q.shape
    dv = v.shape[-1]
    n = s_ // CHUNK

    def to_chunks(t):
        return t.reshape(b_, n, CHUNK, h_, t.shape[-1]).transpose(1, 0, 3, 2, 4)

    causal = jnp.tril(jnp.ones((CHUNK, CHUNK), dtype=bool))[:, :, None]

    def step(state, inp):
        qc, kc, vc, gc = inp
        bcum = jnp.cumsum(gc, axis=2)
        diff = bcum[:, :, :, None, :] - bcum[:, :, None, :, :]
        decay = jnp.where(causal, jnp.exp(jnp.where(causal, diff, 0.0)), 0.0)
        scores = jnp.einsum('bhtd,bhsd,bhtsd->bhts', qc, kc, decay)
        o_intra = jnp.einsum('bhts,bhsv->bhtv', scores, vc)
        o_inter = jnp.einsum('bhtd,bhdv->bhtv', qc * jnp.exp(bcum), state)
        b_last = bcum[:, :, -1, :]
        k_dec = kc * jnp.exp(b_last[:, :, None, :] - bcum)
        new_state = jnp.exp(b_last)[..., None] * state + jnp.einsum('bhsd,bhsv->bhdv', k_dec, vc)
        return new_state, o_intra + o_inter

    s0 = jnp.zeros((b_, h_, dk, dv), jnp.float32)
    _, o = lax.scan(step, s0, (to_chunks(q), to_chunks(k), to_chunks(v), to_chunks(log_a)))
    return o.transpose(1, 0, 3, 2, 4).reshape(b_, s_, h_, dv)

def _causal_depthwise_conv(u, w):
    return lax.conv_general_dilated(
        u, w[:, None, :].astype(u.dtype), window_strides=(1,),
        padding=[(CONV_WIDTH_2 - 1, 0)],
        dimension_numbers=('NWC', 'WIO', 'NWC'),
        feature_group_count=u.shape[-1])

def second_inputs(seed: int = 0) -> dict:
    key = jax.random.key(seed)
    ks = jax.random.split(key, 20)
    nrm = lambda k, shape, scale: jax.random.normal(k, shape, jnp.float32) * scale
    gain = lambda k, shape: 1.0 + 0.05 * jax.random.normal(k, shape, jnp.float32)
    return {
        "x": nrm(ks[0], (BATCH, SEQ, D_MODEL), 1.0),
        "p": nrm(ks[1], (DEPTH_2, BATCH, SEQ, PLE_DIM), 1.0),
        "ln1_g": gain(ks[2], (DEPTH_2, D_MODEL)),
        "w_in": nrm(ks[3], (DEPTH_2, D_MODEL, IN_DIM), D_MODEL ** -0.5),
        "w_gate_up": nrm(ks[4], (DEPTH_2, GATE_RANK, GLA_QK_DIM), GATE_RANK ** -0.5),
        "b_gate": nrm(ks[5], (DEPTH_2, GLA_QK_DIM), 0.1),
        "conv_w": nrm(ks[6], (DEPTH_2, CONV_WIDTH_2, CONV_DIM), CONV_WIDTH_2 ** -0.5),
        "gn_g": gain(ks[7], (DEPTH_2, GLA_DV)),
        "w_out": nrm(ks[8], (DEPTH_2, MIX_DIM, D_MODEL), MIX_DIM ** -0.5),
        "ln2_g": gain(ks[9], (DEPTH_2, D_MODEL)),
        "w_gate_upffn": nrm(ks[10], (DEPTH_2, D_MODEL, 2 * FFN_HIDDEN_2), D_MODEL ** -0.5),
        "w_down": nrm(ks[11], (DEPTH_2, FFN_HIDDEN_2, D_MODEL), FFN_HIDDEN_2 ** -0.5),
        "ln3_g": gain(ks[12], (DEPTH_2, D_MODEL)),
        "w_ple_gate": nrm(ks[13], (DEPTH_2, D_MODEL, D_MODEL), D_MODEL ** -0.5),
        "w_ple_proj": nrm(ks[14], (DEPTH_2, PLE_DIM, D_MODEL), PLE_DIM ** -0.5),
        "lnf_g": gain(ks[15], (D_MODEL,)),
    }

def second_block(x, p, ln1_g, w_in, w_gate_up, b_gate, conv_w, gn_g, w_out, ln2_g,
              w_gate_upffn, w_down, ln3_g, w_ple_gate, w_ple_proj, lnf_g):
    b_, s_, _ = x.shape
    offsets = list(np.cumsum(IN_SPLITS)[:-1])
    h = x
    for i in range(DEPTH_2):
        u = _rmsnorm(h, ln1_g[i])
        proj = u @ w_in[i]
        q, k, v, g, g_lr, cb, cc, cx = jnp.split(proj, offsets, axis=-1)

        gate_logits = (g_lr @ w_gate_up[i] + b_gate[i]).astype(jnp.float32)
        log_a = jax.nn.log_sigmoid(gate_logits) / GATE_NORMALIZER
        qh = q.astype(jnp.float32).reshape(b_, s_, GLA_HEADS, GLA_DK) * (GLA_DK ** -0.5)
        kh = k.astype(jnp.float32).reshape(b_, s_, GLA_HEADS, GLA_DK)
        vh = v.astype(jnp.float32).reshape(b_, s_, GLA_HEADS, GLA_DV)
        ah = log_a.reshape(b_, s_, GLA_HEADS, GLA_DK)
        o = _gla_chunked(qh, kh, vh, ah).astype(x.dtype)
        gh = g.reshape(b_, s_, GLA_HEADS, GLA_DV)
        o = _rmsnorm(o, gn_g[i]) * jax.nn.silu(gh)
        o = o.reshape(b_, s_, GLA_V_DIM)

        y = cb * _causal_depthwise_conv(cc * cx, conv_w[i])

        mix = jnp.concatenate([o, y], axis=-1) @ w_out[i]
        h = h + mix

        u2 = _rmsnorm(h, ln2_g[i])
        a, bb = jnp.split(u2 @ w_gate_upffn[i], 2, axis=-1)
        h = h + (jax.nn.silu(a) * bb) @ w_down[i]

        u3 = _rmsnorm(h, ln3_g[i])
        gate = jax.nn.sigmoid(u3 @ w_ple_gate[i])
        h = h + gate * (p[i] @ w_ple_proj[i])
    return _rmsnorm(h, lnf_g)


def setup_inputs(seed=0):
    out = dict(first_inputs(seed))
    for name, value in second_inputs(seed + 1).items():
        if name != "x":
            out[name + "_2"] = value
    return out


def reference(
    x, mix_norm, ffn_norm, nsa_w_in, cmp_pos_k, cmp_pos_v, cmp_k_w1, cmp_k_w2, cmp_v_w1,
    cmp_v_w2, pool_w, pool_scale, mix_w_out, conv_w_pw1, conv_b_pw1, conv_w_dw, conv_b_dw,
    conv_ln_g, conv_ln_b, conv_w_pw2, conv_b_pw2, ffn_w_gate, ffn_w_up, ffn_w_down, final_norm,
    p_2, ln1_g_2, w_in_2, w_gate_up_2, b_gate_2, conv_w_2, gn_g_2, w_out_2, ln2_g_2,
    w_gate_upffn_2, w_down_2, ln3_g_2, w_ple_gate_2, w_ple_proj_2, lnf_g_2,
):
    x = first_block(
        x, mix_norm, ffn_norm, nsa_w_in, cmp_pos_k, cmp_pos_v, cmp_k_w1, cmp_k_w2, cmp_v_w1,
        cmp_v_w2, pool_w, pool_scale, mix_w_out, conv_w_pw1, conv_b_pw1, conv_w_dw, conv_b_dw,
        conv_ln_g, conv_ln_b, conv_w_pw2, conv_b_pw2, ffn_w_gate, ffn_w_up, ffn_w_down,
        final_norm,
    )
    return second_block(
        x, p_2, ln1_g_2, w_in_2, w_gate_up_2, b_gate_2, conv_w_2, gn_g_2, w_out_2, ln2_g_2,
        w_gate_upffn_2, w_down_2, ln3_g_2, w_ple_gate_2, w_ple_proj_2, lnf_g_2,
    )


_drawn_inputs = setup_inputs


def setup_inputs(seed=0):
    import zlib

    import numpy as np

    out = dict(_drawn_inputs(seed))
    spreads = {}
    factors = {'cmp_pos_k': 8.0,
     'conv_b_pw1': 3.768,
     'conv_ln_b': 4.489,
     'conv_b_pw2': 2.701,
     'b_gate_2': 3.8,
     'gn_g_2': 3.755,
     'ln3_g_2': 27.76}
    for name, (base, spread) in spreads.items():
        noise = np.random.default_rng([zlib.crc32(name.encode()), seed]).standard_normal(out[name].shape)
        drawn = base * np.exp(spread * noise) if base else spread * noise
        out[name] = __import__('jax').numpy.asarray(drawn.astype(out[name].dtype))
    for name, factor in factors.items():
        out[name] = (out[name] * factor).astype(out[name].dtype)
    return out
```

```python
from contextlib import ExitStack

import concourse.bass as bass
from concourse import mybir

F32 = mybir.dt.float32
F32R = mybir.dt.float32r
ALU = mybir.AluOpType
ACT = mybir.ActivationFunctionType
AXX = mybir.AxisListType.X

P = 128
S = 512
TB = S // P
D = 1024
KD = D // P
SLOT = 2048
NH, GR, HPG, DH = 8, 2, 4, 64
NCMP = 31
NCP = 32
FH = 2816
KF = FH // P
KHALF = KF // 2
IN1 = 1816
CONV = 31
CPAD = CONV - 1
PPAD = 16
CH = 64
NCH = S // CH
GH, GDK, GDV = 4, 64, 128
LEVELS = (32, 16, 8, 4, 2, 1)

PHASES = [
    ("q", 2, 2), ("kvc", 1, 2), ("kvs", 1, 2), ("kvw", 1, 2), ("gate", 1, 1), ("u", 2, 2),
    ("ck", 1, 1), ("cv", 1, 1), ("pool", 1, 4), ("mix", 4, 2),
    ("up1", KF, 2), ("dn1", 16, 0.5), ("pw1", 8, 2), ("pw2", 4, 2), ("up2", KF, 2), ("dn2", 16, 0.5),
    ("qk2", 2, 2), ("v2", 2, 2), ("g2", 2, 2), ("glr", 1, 1), ("cb2", 2, 2), ("ccx", 4, 2), ("mix2", 4, 2),
    ("up3", KF, 2), ("dn3", 16, 0.5), ("ple", 8, 2),
]
N0, T0, F0 = {}, {}, {}
_n = _t = _f = 0
for _name, _c, _per in PHASES:
    N0[_name], T0[_name], F0[_name] = _n, _t, _f
    _n, _t = _n + _c, _t + int(_c * _per)
    _f += _c if _per == 2 else 0
NPANEL, NTILE = _n, _t

PARAMS = [("mix_norm", 16), ("ffn_norm", 16), ("final_norm", 8), ("ln1_g_2", 8), ("ln2_g_2", 8), ("ln3_g_2", 8),
          ("lnf_g_2", 8), ("pool_scale", 4), ("conv_b_pw1", 16), ("conv_b_dw", 8), ("conv_ln_g", 8),
          ("conv_ln_b", 8), ("conv_b_pw2", 8), ("b_gate_2", 2), ("gn_g_2", 1)]
COL = {}
_c = 0
for _name, _k in PARAMS:
    COL[_name] = _c
    _c += _k
COL["conv_w_dw"] = P
COL["conv_w_2"] = 3 * P
COL["cmp_pos_k"] = 3 * P + 32
COL["cmp_pos_v"] = 3 * P + 64

NORMS = [COL["mix_norm"], COL["ffn_norm"], COL["mix_norm"] + 8, COL["ffn_norm"] + 8, COL["final_norm"],
         COL["ln1_g_2"], COL["ln2_g_2"], COL["ln3_g_2"], COL["lnf_g_2"]]
NORMS.insert(3, None)
MIX, FFN1, CONVIN, LN, FFN2, FINAL, GLAIN, FFN3, PLE, OUT = range(10)
OFF = {3: 0, 2: 512, 0: 896, 1: 1024}


class Chain:

    def __init__(self, eng, sem):
        self.eng, self.sem, self.base, self.j = eng, sem, 0, 0

    def link(self, ins):
        ins.then_inc(self.sem, 1)
        self.j += 1
        self.eng.wait_ge(self.sem, self.base + self.j)

    def loop(self, i, per):
        self.before = self.base + self.j
        self.base, self.j, self.per = i * per + self.before, 0, per

    def done(self, count):
        assert self.j == self.per, self.j
        self.base, self.j = self.before + count * self.per, 0


def program(nc, t):
    ctx = ExitStack()
    with ctx:
        def sb(name, shape, dt=F32):
            return ctx.enter_context(nc.sbuf_tensor(name, shape, dt))

        sems = {}

        def sem(name):
            if name not in sems:
                sems[name] = ctx.enter_context(nc.semaphore(name))
            return sems[name]

        raw = sb("raw", [P, 2, SLOT])
        whi = sb("whi", [P, 2, SLOT], F32R)
        wlo = sb("wlo", [P, 2, SLOT], F32R)
        x = sb("x", [P, KD, S])
        act_hi = sb("act_hi", [P, KD, S], F32R)
        act_lo = sb("act_lo", [P, KD, S], F32R)
        rstd = sb("rstd", [P, S])
        sq = sb("sq", [P, 2, S])
        sqacc = sb("sqacc", [P, S])
        ones = sb("ones", [P, P])
        ident = sb("ident", [P, P])
        par = sb("par", [P, 4 * P])
        eps6 = sb("eps6", [P, 1])
        eps5 = sb("eps5", [P, 1])
        t1 = sb("t1", [P, 2, S])
        t2 = sb("t2", [P, 2, S])
        t3 = sb("t3", [P, 2, S])
        wtap = sb("wtap", [P, 2, CONV])

        def region(parts):
            got = []
            with ExitStack() as r:
                for name, shape, dt in parts:
                    got.append(r.enter_context(nc.sbuf_tensor(name, shape, dt)))
            return got

        xt, prow = region([("xt", [P, TB, D], F32), ("prow", [P, 4, P], F32)])
        (q_sb, k_sb, vf, v_tm, cmp_hi, cmp_lo, g_tm, kbd, vbd, ghid, w2c, cvalid, pinv, up,
         wsum, dist, slopes, slope_st, biast, q_st, s_sb, pt, acc, mx, nmx, sm, rec, rg, otmp, cmx, csm,
         ) = region([
             ("q_sb", [P, HPG, S], F32), ("k_sb", [P, 2, S], F32), ("vf", [P, 2, S], F32),
             ("v_tm", [P, 2, TB, P], F32), ("cmp_hi", [P, 16, 62], F32R), ("cmp_lo", [P, 16, 62], F32R),
             ("g_tm", [P, TB, 24], F32), ("kbd", [P, 2 * NCP], F32), ("vbd", [P, GR, HPG * DH], F32),
             ("ghid", [P, 2, 62], F32), ("w2c", [P, 2, DH], F32), ("cvalid", [P, TB, NCP], F32), ("pinv", [P, PPAD], F32), ("up", [P, 4, PPAD + S], F32),
             ("wsum", [P, 2, PPAD + S], F32), ("dist", [P, S], F32), ("slopes", [P, NH], F32), ("slope_st", [P, GR], F32),
             ("biast", [P, 2, S], F32), ("q_st", [P, S], F32), ("s_sb", [P, 2, 1280], F32),
             ("pt", [P, 1280], F32), ("acc", [P, TB, NH * DH], F32), ("mx", [P, 2, TB], F32),
             ("nmx", [P, 2, TB], F32), ("sm", [P, 2, TB], F32), ("rec", [P, TB], F32), ("rg", [P, TB], F32),
             ("otmp", [P, TB, DH], F32), ("cmx", [P, 32], F32), ("csm", [P, 32], F32),
         ])
        pc_t = vf
        gsig = t2[0:24, 0]
        cbias = s_sb[:, 1, 0:TB * 256].rearrange("p (b c) -> p b c", b=TB)
        c2 = acc[:, 0:2, :]
        cmpf = acc[:, 2:4, :].rearrange("p b c -> p (b c)")[:, 0:16 * 62].rearrange("p (k n) -> p k n", k=16)
        kvc = pt[:, 0:2 * S].rearrange("p (j t) -> p j t", j=2)
        hid_hi, hid_lo = region([("hid_hi", [P, KF, S], F32R), ("hid_lo", [P, KF, S], F32R)])
        z, zc, mean, zsum = region([("z", [P, 2, CPAD + S], F32), ("zc", [P, KD, S], F32), ("mean", [P, S], F32),
                                 ("zsum", [P, S], F32)])
        (q2, k2, v2f, v2, gs, cbt, ccx, glr, wgu, la, la2, scan1, bc, qkd, glm, kdt, qe) = region([
            ("q2", [P, 2, S], F32), ("k2", [P, 2, S], F32), ("v2f", [P, GH, S], F32),
            ("v2", [P, TB, GH * GDV], F32), ("gs", [P, GH, S], F32), ("cbt", [P, 4, S], F32),
            ("ccx", [P, 4, 2 + S], F32), ("glr", [16, S], F32), ("wgu", [16, 256], F32),
            ("la", [P, 2 * S], F32), ("la2", [P, 2 * S], F32), ("scan1", [P, 2 * S], F32),
            ("bc", [P, 2 * S], F32), ("qkd", [P, 2, 2 * S], F32), ("glm", [P, len(LEVELS), CH], F32),
            ("kdt", [P, TB, 2, P], F32), ("qe", [P, 2 * S], F32),
        ])
        at, dd, ex, osq = v2f, la, scan1, sq[:, 0]
        qd, kd = qkd[:, 0], qkd[:, 1]
        state = qkd[:, :, :].rearrange("p c (n v) -> p c n v", v=GDV)
        yt, ptok, pf_hi, pf_lo = region([("yt", [P, TB, D], F32), ("ptok", [P, TB, 256], F32),
                                         ("pf_hi", [P, 2, S], F32R), ("pf_lo", [P, 2, S], F32R)])

        ps = [ctx.enter_context(nc.psum_tensor(f"ps{i}", [P, S], F32)) for i in range(8)]

        raw_full = [sem("raw_full0"), sem("raw_full1")]
        hi_done, split_done = sem("hi_done"), sem("split_done")
        panel_done, tile_done, bank_free = sem("panel_done"), sem("tile_done"), sem("bank_free")

        def bank(tile):
            return ps[tile % 4]

        block = ctx.enter_context(nc.Block())

        @block.sync
        def _(sp):
            def load(n, slot, halves):
                if not (isinstance(n, int) and n < 2):
                    sp.wait_ge(split_done, n - 1)
                for dst, src in halves:
                    sp.dma_start(dst, src).then_inc(raw_full[slot], 16)

            def slot8(s):
                return raw[:, s].rearrange("p (k j c) -> p k j c", k=KD, j=2)

            def cols256(w, c0, s):
                v = w.rearrange("(k p) n -> p k n", p=P)
                r = raw[:, s].rearrange("p (k c) -> p k c", k=KD)
                return [(r[:, 0:4, :], v[:, 0:4, c0]), (r[:, 4:8, :], v[:, 4:8, c0])]

            def pair(w, c0, c1, s):
                v = w.rearrange("(k p) n -> p k n", p=P)
                r = slot8(s)
                return [(r[:, :, 0, :], v[:, :, c0]), (r[:, :, 1, :], v[:, :, c1])]

            def straight(name, count, halves):
                for i in range(count):
                    n = N0[name] + i
                    load(n, n % 2, halves(i, n % 2))

            def looped(name, count, halves):
                with sp.Fori(0, count // 2) as i:
                    for j in range(2):
                        n = N0[name] + j
                        load(2 * i + n, n % 2, halves(2 * i + j, n % 2))

            sp.dma_start(ident[:, :], t["ident"]).then_inc(sem("ident_in"), 16)
            for b in range(TB):
                sp.dma_start(xt[:, b, :], t["x"][0, b * P:(b + 1) * P, :]).then_inc(sem("x_in"), 16)
            w = t["nsa_w_in"][0]
            straight("q", 2, lambda i, s: [
                (raw[:, s].rearrange("p (k r g c) -> p k r g c", k=KD, r=2, g=2)[:, :, r, g, :],
                 w.rearrange("(k p) n -> p k n", p=P)[:, :, (g * HPG + 2 * i + r) * DH:(g * HPG + 2 * i + r + 1) * DH])
                for r in range(2) for g in range(2)])
            for j, name in enumerate(("kvc", "kvs", "kvw")):
                straight(name, 1, lambda i, s: cols256(w, bass.ds(512 + 256 * j, 256), s))
            straight("gate", 1, lambda i, s: [
                (slot8(s)[:, a:a + 4, 0, 0:24], w.rearrange("(k p) n -> p k n", p=P)[:, a:a + 4, 1280:1304])
                for a in (0, 4)])
            straight("u", 2, lambda i, s: cols256(w, bass.ds(1304 + 256 * i, 256), s))
            for name in ("ck", "cv"):
                w1 = t["cmp_k_w1" if name == "ck" else "cmp_v_w1"][0].rearrange("(k p) n -> p k n", p=P)
                straight(name, 1, lambda i, s: [
                    (raw[:, s].rearrange("p (k c) -> p k c", c=P)[:, a:a + 8], w1[:, a:a + 8]) for a in (0, 8)])
            straight("pool", 1, lambda i, s: [
                (raw[:, s, 0:512].rearrange("p (g e) -> p g e", g=4)[:, a:a + 2],
                 t["pool_w"][0].rearrange("g c e -> c g e")[:, a:a + 2]) for a in (0, 2)])
            looped("mix", 4, lambda i, s: cols256(t["mix_w_out"][0], bass.ds(i * 256, 256), s))

            def ffn(up, dn, wg, wu, wd, off):
                looped(up, KF, lambda i, s: pair2(wg, bass.ds(i * 128, 128), wu, bass.ds(off + i * 128, 128), s))
                wdv = wd.rearrange("(h k p) n -> p h k n", p=P, h=2)
                r = [raw[:, s, 0:KHALF * P].rearrange("p (k c) -> p k c", k=KHALF) for s in range(2)]
                n = N0[dn]
                with sp.Fori(0, KD) as m:
                    for h in range(2):
                        s = (n + h) % 2
                        load(2 * m + n + h, s, [
                            (r[s][:, 0:6, :], wdv[:, h, 0:6, bass.ds(m * P, P)]),
                            (r[s][:, 6:KHALF, :], wdv[:, h, 6:KHALF, bass.ds(m * P, P)])])

            def pair2(wa, c0, wb, c1, s):
                r = slot8(s)
                return [(r[:, :, 0, :], wa.rearrange("(k p) n -> p k n", p=P)[:, :, c0]),
                        (r[:, :, 1, :], wb.rearrange("(k p) n -> p k n", p=P)[:, :, c1])]

            ffn("up1", "dn1", t["ffn_w_gate"][0], t["ffn_w_up"][0], t["ffn_w_down"][0], 0)
            w = t["conv_w_pw1"][0]
            looped("pw1", 8, lambda i, s: pair(w, bass.ds(i * 128, 128), bass.ds(i * 128 + D, 128), s))
            looped("pw2", 4, lambda i, s: cols256(t["conv_w_pw2"][0], bass.ds(i * 256, 256), s))
            ffn("up2", "dn2", t["ffn_w_gate"][1], t["ffn_w_up"][1], t["ffn_w_down"][1], 0)
            w2 = t["w_in_2"][0]
            straight("qk2", 2, lambda i, s: cols256(w2, bass.ds(256 * i, 256), s))
            straight("v2", 2, lambda i, s: cols256(w2, bass.ds(512 + 256 * i, 256), s))
            straight("g2", 2, lambda i, s: cols256(w2, bass.ds(1024 + 256 * i, 256), s))
            straight("glr", 1, lambda i, s: [
                (slot8(s)[:, a:a + 4, 0, 0:16], w2.rearrange("(k p) n -> p k n", p=P)[:, a:a + 4, 1536:1552])
                for a in (0, 4)])
            straight("cb2", 2, lambda i, s: cols256(w2, bass.ds(1552 + 256 * i, 256), s))
            looped("ccx", 4, lambda i, s: pair(w2, bass.ds(i * 128 + 2064, 128), bass.ds(i * 128 + 2576, 128), s))
            looped("mix2", 4, lambda i, s: cols256(t["w_out_2"][0], bass.ds(i * 256, 256), s))
            ffn("up3", "dn3", t["w_gate_upffn_2"][0], t["w_gate_upffn_2"][0], t["w_down_2"][0], FH)

            def ple(i, s):
                r = raw[:, s, 0:1280].rearrange("p (k c) -> p k c", c=P)
                return [(r[:, 0:8], t["w_ple_gate_2"][0].rearrange("(k p) n -> p k n", p=P)[:, :, bass.ds(i * P, P)]),
                        (r[:, 8:10], t["w_ple_proj_2"][0].rearrange("(k p) n -> p k n", p=P)[:, :, bass.ds(i * P, P)])]
            looped("ple", 8, ple)
            for b in range(TB):
                sp.wait_ge(sem("y_copied"), 2 * b + 2)
                sp.dma_start(t["out"][0, b * P:(b + 1) * P, :], yt[:, b, :]).then_inc(sem("y_out"), 16)
            sp.wait_ge(sem("y_out"), 16 * TB)

        @block.gpsimd
        def _(pool):
            pool.memset(prow[:, :, :], 0.0).then_inc(sem("prow_zero"), 1)
            pool.memset(ones[:, :], 1.0).then_inc(sem("ones_set"), 1)
            pool.wait_ge(sem("prow_zero"), 1)
            for name, rows in PARAMS:
                src = t[name].rearrange("a b -> (a b)") if len(t[name].shape) == 2 else t[name]
                pool.dma_start(prow[COL[name]:COL[name] + rows, 0, :],
                               src.rearrange("(r c) -> r c", c=P)).then_inc(sem("params_in"), 16)
            taps = t["conv_w_dw"][0].rearrange("j (m c) -> (j m) c", c=P)
            pool.dma_start(prow[:, 1, :], taps[0:P]).then_inc(sem("params_in"), 16)
            pool.dma_start(prow[0:CONV * KD - P, 2, :], taps[P:CONV * KD]).then_inc(sem("params_in"), 16)
            pool.dma_start(prow[0:12, 3, :], t["conv_w_2"][0].rearrange("j (m c) -> (j m) c", c=P))\
                .then_inc(sem("params_in"), 16)
            for name, row in (("cmp_pos_k", 32), ("cmp_pos_v", 64)):
                pool.dma_start(prow[row:row + 16, 3, :], t[name][0].rearrange("(j b) c -> j (b c)", b=2))\
                    .then_inc(sem("params_in"), 16)

            pool.wait_ge(sem("setup_copied"), 1 + KD)
            pool.memset(up[:, :, 0:PPAD], 0.0).then_inc(sem("att_zero"), 1)
            pool.memset(kbd[:, :], 0.0).then_inc(sem("att_zero"), 1)
            pool.memset(vbd[:, :, :], 0.0).then_inc(sem("att_zero"), 1)
            for dst, src in ((w2c[:, 0], t["cmp_k_w2"][0]), (w2c[:, 1], t["cmp_v_w2"][0]), (cbias[:, :, :], t["cbias"]),
                             (cvalid[:, :, :], t["cvalid"]), (dist[:, :], t["dist"]), (slopes[:, :], t["slopes"]),
                             (pinv[:, :], t["pinv"])):
                pool.dma_start(dst, src).then_inc(sem("att_consts"), 16)
            pool.wait_ge(sem("att_consts"), 16 * 7)
            pool.wait_ge(sem("att_zero"), 1)

            own = Chain(pool, sem("pool_seq"))

            def stage(u, r, g, first):
                if not first:
                    pool.wait_ge(sem("s_ready"), u - 1)
                    pool.wait_ge(sem("nmax_ready"), u - 1)
                h = slice(g * DH, (g + 1) * DH)
                own.link(pool.tensor_copy(slope_st[:, g:g + 1], slopes[:, bass.ds(r + g * HPG, 1)]))
                own.link(pool.tensor_copy(q_st[h, :], q_sb[h, bass.ds(r, 1), :]))
                pool.tensor_tensor(biast[:, g, :], dist[:, :], slope_st[:, g:g + 1].broadcast_to([P, S]), ALU.mult)\
                    .then_inc(sem("staged"), 1)

            def stage_rest(b):
                with pool.Fori(0, HPG - 1) as r:
                    own.loop(r, 2 * GR)
                    for g in range(GR):
                        stage(2 * r + (8 * b + g + 2), r + 1, g, False)
                    own.done(HPG - 1)

            pool.wait_ge(bank_free, T0["q"] + 8)
            for g in range(GR):
                stage(g, 0, g, True)

            for gi in range(4):
                pool.wait_ge(bank_free, T0["u"] + gi + 5)
                src, lo, w = up[:, gi], 0, 2 << gi
                for lev in range(gi + 1):
                    step = 1 << lev
                    lo += step
                    dst = wsum[:, lev % 2]
                    own.link(pool.tensor_tensor(dst[:, lo:], src[:, lo:], src[:, lo - step:PPAD + S - step], ALU.add))
                    src = dst
                pool.tensor_scalar(src[:, PPAD + w:], src[:, PPAD + w:], 1.0 / w, None, ALU.mult)
                own.link(pool.tensor_tensor(src[:, PPAD:PPAD + w], src[:, PPAD:PPAD + w], pinv[:, 0:w], ALU.mult))
                pool.tensor_tensor(up[:, gi, PPAD:], src[:, PPAD:], up[:, gi, PPAD:], ALU.subtract)\
                    .then_inc(sem("d_ready"), 1)
                pool.wait_ge(sem("d_ready"), gi + 1)
            stage_rest(0)
            for g in range(GR):
                stage(8 + g, 0, g, False)
            stage_rest(1)

            pool.wait_ge(bank_free, T0["qk2"] + 4)
            pool.dma_start(wgu[:, :], t["w_gate_up_2"][0]).then_inc(sem("gla_consts"), 16)
            pool.dma_start(glm[:, :, :], t["glm"]).then_inc(sem("gla_consts"), 16)
            pool.memset(scan1[:, :], 1.0).then_inc(sem("gla_set"), 1)
            pool.memset(ccx[:, :, 0:2], 0.0).then_inc(sem("gla_set"), 1)
            pool.wait_ge(sem("gla_set"), 2)
            pool.memset(scan1[:, :].rearrange("p (c t) -> p c t", t=CH)[:, :, 0:1], 0.0).then_inc(sem("gla_set"), 1)

            pool.wait_ge(panel_done, N0["ple"])
            pool.dma_start(ptok[:, :, :], t["p_2"][0, 0].rearrange("(b p) c -> p b c", p=P))\
                .then_inc(sem("p_in"), 16)

        @block.scalar
        def _(act):
            seq = Chain(act, sem("act_seq"))

            def hi(n, i=0):
                act.wait_ge(raw_full[n % 2], 32 * i + 32 * (n // 2 + 2))
                if n >= 2:
                    act.wait_ge(panel_done, 2 * i + (n - 1))
                act.activation(whi[:, n % 2], raw[:, n % 2], ACT.Copy).then_inc(hi_done, 1)

            def square(q, k, src, kk=None):
                if q or k >= 2:
                    act.wait_ge(sem("sq_added"), k + (8 * q - 1))
                act.activation(sq[:, (k if kk is None else kk) % 2], src, ACT.Square).then_inc(sem("sq_ready"), 1)

            def cast(dst, src, name, scale=1.0):
                act.activation(dst, src, ACT.Copy, scale=scale).then_inc(sem(name), 1)

            def gain(q, k):
                return par[:, bass.ds(NORMS[q] + k, 1)]

            def root(q):
                act.wait_ge(sem("sumsq"), q + 1)
                act.activation(rstd[:, :], ps[4][:, :], ACT.Sqrt, bias=(eps5 if q == LN else eps6)[:, :],
                               scale=1.0 / D).then_inc(sem("std_ready"), 1)

            hi(0)
            act.wait_ge(sem("consts_set"), 1)
            for k in range(2):
                act.wait_ge(sem("setup_copied"), k + 1)
                square(MIX, k, x[:, k])
            act.wait_ge(sem("setup_copied"), KD + 1)
            for k in range(KD):
                cast(act_hi[:, k], x[:, k], f"xhi{MIX}", gain(MIX, k))
                if k >= 2:
                    square(MIX, k, x[:, k])
            root(MIX)

            for name, count, _ in PHASES[:4]:
                for i in range(count):
                    hi(N0[name] + i + 1)
            hi(N0["gate"] + 1)
            act.wait_ge(bank_free, T0["gate"] + 5)
            act.activation(gsig, t1[0:24, 0], ACT.Sigmoid).then_inc(sem("gate_sig"), 1)
            for i in range(2):
                hi(N0["u"] + i + 1)
            for j, name in enumerate(("ck", "cv")):
                act.wait_ge(sem("cmp_set"), j + 1)
                if j:
                    act.wait_ge(panel_done, N0["cv"])
                cast(cmp_hi[:, :, :], cmpf[:, :, :], "cmp_hi")
                hi(N0[name] + 1)
                act.wait_ge(bank_free, T0[name] + 5)
                act.activation(ghid[:, j], t1[:, j, 0:62], ACT.Gelu_apprx_tanh).then_inc(sem("ghid_ready"), 1)
            act.wait_ge(sem("c_shifted"), 1)
            act.activation(s_sb[:, 0, 0:1024], s_sb[:, 0, 0:1024], ACT.Exp).then_inc(sem("c_exp"), 1)
            act.wait_ge(sem("c_pv"), 2)
            act.activation(acc[:, 1], ps[1][:, :], ACT.Copy)
            act.wait_ge(sem("c_pv"), 4)
            act.activation(acc[:, 3], ps[3][:, :], ACT.Copy).then_inc(sem("pt_a"), 1)

            def exps(u, g):
                act.wait_ge(sem("nmax_ready"), u + 1)
                for qb in range(TB):
                    w = (qb + 1) * P
                    e = s_sb[:, g, OFF[qb]:OFF[qb] + w]
                    ins = act.activation(e, e, ACT.Exp, bias=nmx[:, g, qb:qb + 1], accum_out=sm[:, g, qb:qb + 1])
                ins.then_inc(sem("p_ready"), 1)

            def copy_pt(u):
                act.wait_ge(sem("pt_ready"), 3 * u + 1)
                act.wait_ge(sem("pv_ready"), u + 1)
                act.activation(pt[:, 0:512], ps[6][:, :], ACT.Copy).then_inc(sem("pt_a"), 1)
                act.wait_ge(sem("pt_ready"), 3 * u + 3)
                act.activation(pt[:, 1024:1280], ps[6][:, 0:256], ACT.Copy).then_inc(sem("pt_a"), 1)

            for b in range(2):
                for g in range(GR):
                    exps(8 * b + g, g)
                with act.Fori(0, HPG - 1) as r:
                    for g in range(GR):
                        copy_pt(2 * r + (8 * b + g))
                        exps(2 * r + (8 * b + g + 2), g)
                for g in range(GR):
                    copy_pt(8 * b + 6 + g)
            for gi in range(4):
                act.wait_ge(sem("d_ready"), gi + 1)
                cast(act_hi[:, 4 + gi], up[:, gi, PPAD:], "d_hi")
            hi(N0["pool"] + 1)
            for k in range(4):
                act.wait_ge(sem("oT_ready"), k + 1)
                cast(act_hi[:, k], ps[4 + k][:, :], "o_hi")
            for gi in range(4):
                act.wait_ge(bank_free, T0["pool"] + gi + 5)
                cast(act_hi[:, 4 + gi], t1[:, gi % 2], "y_hi")

            def late(q, name, extra=None):
                for i in range(4):
                    hi(N0[name] + i + 1)
                    for k in (2 * i, 2 * i + 1):
                        act.wait_ge(bank_free, T0[name] + k + 5)
                        square(q, k, x[:, k])
                act.wait_ge(panel_done, N0[name] + 4)
                for k in range(KD):
                    cast(act_hi[:, k], x[:, k], f"xhi{q}", gain(q, k))

            late(FFN1, "mix")

            def ffn(f, q, up_, dn, qn):
                root(q)
                with act.Fori(0, KF // 2) as i:
                    for j in range(2):
                        hi(N0[up_] + j + 1, i)
                        act.wait_ge(bank_free, 4 * i + (T0[up_] + 2 * j + 5))
                        act.activation(t3[:, j], t1[:, j], ACT.Silu).then_inc(sem("silu_ready"), 1)
                        act.wait_ge(sem("hidden_set"), 2 * i + (KF * f + j + 1))
                        cast(hid_hi[:, bass.ds(2 * i + j, 1), :], t1[:, j], "hidden_hi")
                with act.Fori(0, 2) as i:
                    for j in range(4):
                        for h in range(2):
                            hi(N0[dn] + 2 * j + h + 1, 4 * i)
                        act.wait_ge(bank_free, 4 * i + (T0[dn] + j + 5))
                        square(qn, 4 * i + j, x[:, bass.ds(4 * i + j, 1), :], j)
                        if qn != FINAL:
                            cast(act_hi[:, bass.ds(4 * i + j, 1), :], x[:, bass.ds(4 * i + j, 1), :],
                                 f"xhi{qn}", gain(qn, 4 * i + j))

            ffn(0, FFN1, "up1", "dn1", CONVIN)

            root(CONVIN)
            with act.Fori(0, 4) as i:
                for j in range(2):
                    hi(N0["pw1"] + j + 1, i)
                    act.wait_ge(bank_free, 4 * i + (T0["pw1"] + 2 * j + 6))
                    act.activation(t3[:, j], t2[:, j], ACT.Sigmoid,
                                   bias=par[:, bass.ds(2 * i + (COL["conv_b_pw1"] + 8 + j), 1)])\
                        .then_inc(sem("glu_sig"), 1)
            for k in range(KD):
                act.wait_ge(sem("ln_centered"), k + 1)
                square(LN, k, zc[:, k])
            root(LN)
            for k in range(KD):
                act.wait_ge(sem("ln_scaled"), k + 1)
                seq.link(act.activation(t3[:, k % 2], t1[:, k % 2], ACT.Silu,
                                        scale=par[:, COL["conv_ln_g"] + k:COL["conv_ln_g"] + k + 1],
                                        bias=par[:, COL["conv_ln_b"] + k:COL["conv_ln_b"] + k + 1]))
                cast(act_hi[:, k], t3[:, k % 2], "zhi")
            late(FFN2, "pw2")
            ffn(1, FFN2, "up2", "dn2", FINAL)
            root(FINAL)
            for k in range(KD):
                act.wait_ge(sem("x_final"), k + 1)
                square(GLAIN, k, x[:, k])
                cast(act_hi[:, k], x[:, k], f"xhi{GLAIN}", gain(GLAIN, k))
            root(GLAIN)

            for name in ("qk2", "v2"):
                for i in range(2):
                    hi(N0[name] + i + 1)
            for i in range(2):
                hi(N0["g2"] + i + 1)
                for j in range(2):
                    act.wait_ge(bank_free, T0["g2"] + 2 * i + j + 5)
                    act.activation(gs[:, 2 * i + j], gs[:, 2 * i + j], ACT.Silu).then_inc(sem("gs_ready"), 1)
            hi(N0["glr"] + 1)
            for i in range(2):
                hi(N0["cb2"] + i + 1)
            for i in range(4):
                hi(N0["ccx"] + i + 1)
            act.wait_ge(sem("logit_ready"), 2)
            seq.link(act.activation(la2[:, :], la[:, :], ACT.Abs))
            seq.link(act.activation(la2[:, :], la2[:, :], ACT.Exp, scale=-1.0))
            act.activation(la2[:, :], la2[:, :], ACT.Ln, bias=1.0).then_inc(sem("softplus_ready"), 1)
            for lev in range(len(LEVELS)):
                act.wait_ge(sem("dd_ready"), lev + 1)
                seq.link(act.activation(ex[:, :], dd[:, :], ACT.Abs))
                act.activation(ex[:, :], ex[:, :], ACT.Exp, scale=-1.0).then_inc(sem("ex_ready"), 1)
            act.wait_ge(sem("dd_ready"), len(LEVELS) + 1)
            act.wait_ge(sem("kd_ready"), len(LEVELS))
            act.activation(ex[:, :], dd[:, :], ACT.Exp).then_inc(sem("ex_ready"), 1)
            act.activation(la2[:, :], bc[:, :], ACT.Exp).then_inc(sem("ebc_ready"), 1)
            for h in range(GH):
                act.wait_ge(sem("go_ready"), h + 1)
                if h:
                    act.wait_ge(sem("go_sum"), h)
                act.activation(osq, ps[4 + h][:, :], ACT.Square).then_inc(sem("osq_ready"), 1)
            for h in range(GH):
                act.wait_ge(sem("go_sum"), h + 1)
                act.wait_ge(sem("go_rstd"), h) if h else None
                act.activation(t3[:, h % 2], ps[h][:, :], ACT.Sqrt, bias=eps6[:, :], scale=1.0 / GDV)\
                    .then_inc(sem("go_std"), 1)
                act.wait_ge(sem("go_out"), h + 1)
                cast(act_hi[:, h], t1[:, h % 2], "go_hi")
            for k in range(4):
                act.wait_ge(sem("yc_ready"), k + 1)
                cast(act_hi[:, 4 + k], cbt[:, k], "yc_hi")
            late(FFN3, "mix2")
            ffn(2, FFN3, "up3", "dn3", PLE)

            root(PLE)
            for c in range(2):
                act.wait_ge(sem("pf_ready"), c + 1)
                cast(pf_hi[:, c], ps[5 + c][:, :], "pf_hi")

            def ple(i, j, more):
                if more:
                    hi(N0["ple"] + j + 1, i)
                act.wait_ge(bank_free, 4 * i + (T0["ple"] + 2 * j + 5))
                act.activation(t3[:, j], t1[:, j], ACT.Sigmoid).then_inc(sem("ple_sig"), 1)
                act.wait_ge(sem("ple_x"), 2 * i + (j + 1))
                square(OUT, 2 * i + j, x[:, bass.ds(2 * i + j, 1), :], j)

            with act.Fori(0, 3) as i:
                for j in range(2):
                    ple(i, j, True)
            ple(3, 0, True)
            ple(3, 1, False)
            root(OUT)

        @block.tensor
        def _(pe):
            def mm3(out, lhs, rhs, start, stop):
                pe.matmul(out, lhs[0], rhs[0], start=start, stop=False)
                pe.matmul(out, lhs[0], rhs[1], start=False, stop=False)
                return pe.matmul(out, lhs[1], rhs[0], start=False, stop=stop)

            def slot(n, k, width=256, c0=0):
                a = slice(k * width + c0, k * width + c0 + P)
                return whi[:, n % 2, a], wlo[:, n % 2, a]

            def act_k(k):
                return act_hi[:, k], act_lo[:, k]

            def tile(T, i4, lhs, rhs, ks, sig, start=True, stop=True, act_wait=None):
                if start:
                    pe.wait_ge(bank_free, i4 + (T + 1))
                for k in ks:
                    if act_wait:
                        pe.wait_ge(sem(act_wait), k + 1)
                    ins = mm3(bank(T)[:, :], lhs(k), rhs(k), start and k == ks[0], stop and k == ks[-1])
                ins.then_inc(sig, 1)

            def panel2(name, j, i=0, lhs=None, act_wait=None, after=None):
                n, T = N0[name] + j, T0[name] + 2 * j
                pe.wait_ge(split_done, 2 * i + (n + 1))
                for c in range(2):
                    f = lhs(n, c) if lhs else (lambda k: slot(n, k, 256, c * P))
                    tile(T + c, 4 * i, f, act_k, range(KD), panel_done if c else tile_done,
                         act_wait=act_wait if c == 0 else None)
                    if c == 0 and after:
                        after()

            def sumsq(q):
                pe.wait_ge(sem("sq_added"), 8 * q + 8)
                pe.matmul(ps[4][:, :], ones[:, :], sqacc[:, :], start=True, stop=True).then_inc(sem("sumsq"), 1)

            pe.wait_ge(sem("ident_in"), 16)
            pe.wait_ge(sem("x_in"), 16 * TB)
            for k in range(KD):
                if k >= 4:
                    pe.wait_ge(sem("setup_copied"), k - 3)
                for b in range(TB):
                    ins = pe.transpose(ps[4 + k % 4][:, b * P:(b + 1) * P], xt[:, b, k * P:(k + 1) * P], ident[:, :])
                ins.then_inc(sem("setup_ready"), 1)
            pe.wait_ge(sem("params_in"), 16 * (len(PARAMS) + 5))
            pe.wait_ge(sem("setup_copied"), 5)
            for b in range(4):
                ins = pe.transpose(ps[4][:, b * P:(b + 1) * P], prow[:, b], ident[:, :])
            ins.then_inc(sem("setup_ready"), 1)

            pe.wait_ge(sem("ones_set"), 1)
            for i in range(2):
                panel2("q", i, act_wait=f"act{MIX}" if i == 0 else None,
                       after=(lambda: sumsq(MIX)) if i == 0 else None)
            panel2("kvc", 0)
            for br, name in enumerate(("kvs", "kvw")):
                panel2(name, 0)
                pe.wait_ge(bank_free, T0[name] + 6)
                for kb in range(TB):
                    ins = pe.transpose(ps[5 + br][:, kb * P:(kb + 1) * P], vf[:, br, kb * P:(kb + 1) * P], ident[:, :])
                ins.then_inc(sem("vT_ready"), 1)
            n = N0["gate"]
            pe.wait_ge(split_done, n + 1)
            tile(T0["gate"], 0, lambda k: slot(n, k), act_k, range(KD), panel_done)
            panel2("u", 0)
            pe.wait_ge(sem("gate_sig"), 1)
            for b in range(TB):
                ins = pe.transpose(ps[7][:, b * 24:(b + 1) * 24], gsig[:, b * P:(b + 1) * P], ident[0:24, 0:24])
            ins.then_inc(sem("gT_ready"), 1)
            panel2("u", 1)

            for j, name in enumerate(("ck", "cv")):
                n, T = N0[name], T0[name]
                pe.wait_ge(split_done, n + 1)
                pe.wait_ge(sem("cmp_lo"), j + 1)
                pe.wait_ge(bank_free, T + 1)
                for k in range(16):
                    ins = mm3(bank(T)[:, 0:62], slot(n, k, P), (cmp_hi[:, k], cmp_lo[:, k]), k == 0, k == 15)
                ins.then_inc(panel_done, 1)
                pe.wait_ge(sem("ghid_ready"), j + 1)
                pe.wait_ge(sem("att_consts"), 16 * 7)
                if j == 0:
                    pe.matmul(ps[4][0:DH, 0:62], w2c[:, 0], ghid[:, 0], start=True, stop=True)\
                        .then_inc(sem("kcmp_ready"), 1)
                else:
                    for g in range(GR):
                        ins = pe.matmul(ps[5][0:NCMP, g * DH:(g + 1) * DH], ghid[:, 1, g * NCMP:(g + 1) * NCMP],
                                        w2c[:, 1], start=True, stop=True)
                    ins.then_inc(sem("vcmp_ready"), 1)
            pe.wait_ge(sem("kbd_ready"), 1)
            pe.wait_ge(sem("vbd_ready"), 1)
            pe.wait_ge(bank_free, T0["pool"] + 4)
            for b in range(TB):
                for r in range(HPG):
                    out = ps[b // 2][:, (b % 2) * 256:(b % 2 + 1) * 256].rearrange("p (g r n) -> p g r n", g=GR, r=HPG)
                    ins = pe.matmul(out[:, :, r, :], q_sb[:, r, b * P:(b + 1) * P], kbd[:, :],
                                    start=True, stop=True)
            ins.then_inc(sem("c_scores"), 1)
            pe.wait_ge(sem("c_probs"), 1)
            for g in range(GR):
                for b in range(TB):
                    ins = pe.transpose(ps[6 + g][:, b * P:(b + 1) * P],
                                       s_sb[:, 0, b * 256 + g * P:b * 256 + (g + 1) * P], ident[:, :])
            ins.then_inc(sem("c_pT"), 1)
            pe.wait_ge(sem("c_pT_copied"), 1)
            for b in range(TB):
                for g in range(GR):
                    ins = pe.matmul(ps[b][:, g * 256:(g + 1) * 256], pc_t[:, g, b * P:(b + 1) * P], vbd[:, g],
                                    start=True, stop=True)
                ins.then_inc(sem("c_pv"), 1)

            def scores(u, b, g):
                pe.wait_ge(sem("staged"), u + 1)
                h = slice(g * DH, (g + 1) * DH)
                for qb, bk, c in ((3, 0, 0), (2, 1, 0), (0, 1, 384), (1, 2, 0)):
                    ins = pe.matmul(ps[3 * g + bk][:, c:c + (qb + 1) * P], q_st[h, qb * P:(qb + 1) * P],
                                    k_sb[h, b, 0:(qb + 1) * P], start=True, stop=True)
                ins.then_inc(sem("s_ready"), 1)

            def output(u, b, g):
                def pT(kb, bk, c):
                    for qb in range(kb, TB):
                        o = OFF[qb] + kb * P
                        ins = pe.transpose(ps[bk][:, c + (qb - kb) * P:c + (qb - kb + 1) * P],
                                           s_sb[:, g, o:o + P], ident[:, :])
                    return ins
                pe.wait_ge(sem("p_ready"), u + 1)
                pe.wait_ge(sem("pt_a"), 2 * u + 1)
                pT(0, 6, 0).then_inc(sem("pt_ready"), 1)
                pe.wait_ge(sem("pv_out"), u + 1)
                pT(1, 7, 0)
                pT(3, 7, 384).then_inc(sem("pt_ready"), 1)
                pe.wait_ge(sem("pt_a"), 2 * u + 2)
                pT(2, 6, 0).then_inc(sem("pt_ready"), 1)
                pe.wait_ge(sem("pt_v"), u + 1)
                pe.wait_ge(sem("pt_a"), 2 * u + 3)
                start_of = {0: 0, 1: 512, 3: 896, 2: 1024}
                for qb in range(TB):
                    for kb in range(qb + 1):
                        o = start_of[kb] + (qb - kb) * P
                        ins = pe.matmul(ps[7][:, qb * DH:(qb + 1) * DH], pt[:, o:o + P],
                                        v_tm[:, b, kb, g * DH:(g + 1) * DH], start=kb == 0, stop=kb == qb)
                ins.then_inc(sem("pv_ready"), 1)

            pe.wait_ge(sem("c_done"), 1)
            pe.wait_ge(sem("pt_a"), 1)
            for b in range(2):
                for g in range(GR):
                    scores(8 * b + g, b, g)
                with pe.Fori(0, HPG - 1) as r:
                    for g in range(GR):
                        output(2 * r + (8 * b + g), b, g)
                        scores(2 * r + (8 * b + g + 2), b, g)
                for g in range(GR):
                    output(8 * b + 6 + g, b, g)

            n = N0["pool"]
            pe.wait_ge(split_done, n + 1)
            for gi in range(4):
                pe.wait_ge(sem("d_lo"), gi + 1)
                pe.wait_ge(bank_free, T0["pool"] + gi + 1)
                ins = mm3(bank(T0["pool"] + gi)[:, :], slot(n, gi, P), act_k(4 + gi), True, True)
            ins.then_inc(panel_done, 1)
            pe.wait_ge(sem("pv_out"), 17)
            for k in range(4):
                for b in range(TB):
                    ins = pe.transpose(ps[4 + k][:, b * P:(b + 1) * P], acc[:, b, k * P:(k + 1) * P], ident[:, :])
                ins.then_inc(sem("oT_ready"), 1)

            pe.wait_ge(sem("o_lo"), 4)
            pe.wait_ge(sem("y_lo"), 4)
            with pe.Fori(0, 2) as i:
                for j in range(2):
                    panel2("mix", j, i)

            def ffn(f, q, up_, dn):
                panel2(up_, 0, act_wait=f"act{q}", after=lambda: sumsq(q))
                panel2(up_, 1)
                with pe.Fori(1, KF // 2) as i:
                    for j in range(2):
                        panel2(up_, j, i)
                n, T = N0[dn], T0[dn]
                with pe.Fori(0, 2) as i:
                    for j in range(4):
                        for h in range(2):
                            m = n + 2 * j + h
                            pe.wait_ge(split_done, 8 * i + (m + 1))
                            pe.wait_ge(sem("hidden_lo"), KF * f + KHALF * (h + 1))
                            tile(T + j, 4 * i, lambda k: slot(m, k, P),
                                 lambda k: (hid_hi[:, h * KHALF + k], hid_lo[:, h * KHALF + k]),
                                 range(KHALF), panel_done, start=h == 0, stop=h == 1)

            ffn(0, FFN1, "up1", "dn1")

            panel2("pw1", 0, act_wait=f"act{CONVIN}", after=lambda: sumsq(CONVIN))
            panel2("pw1", 1)
            with pe.Fori(1, 4) as i:
                for j in range(2):
                    panel2("pw1", j, i)
            pe.wait_ge(sem("zsum_ready"), 1)
            pe.matmul(ps[5][:, :], ones[:, :], zsum[:, :], start=True, stop=True).then_inc(sem("zmean_ready"), 1)
            sumsq(LN)
            panel2("pw2", 0, act_wait="zlo")
            panel2("pw2", 1)
            with pe.Fori(1, 2) as i:
                for j in range(2):
                    panel2("pw2", j, i)
            ffn(1, FFN2, "up2", "dn2")

            sumsq(FINAL)
            panel2("qk2", 0, act_wait=f"act{GLAIN}", after=lambda: sumsq(GLAIN))
            panel2("qk2", 1)
            for name in ("v2", "g2"):
                for j in range(2):
                    panel2(name, j)
            n = N0["glr"]
            pe.wait_ge(split_done, n + 1)
            tile(T0["glr"], 0, lambda k: slot(n, k), act_k, range(KD), panel_done)
            pe.wait_ge(bank_free, T0["g2"] + 4)
            for w in range(TB):
                for h in range(GH):
                    ins = pe.transpose(ps[4 + w][:, h * P:(h + 1) * P], v2f[:, h, w * P:(w + 1) * P], ident[:, :])
                ins.then_inc(sem("v2T_ready"), 1)
            for j in range(2):
                panel2("cb2", j)
            pe.wait_ge(bank_free, T0["glr"] + 5)
            pe.wait_ge(sem("gla_consts"), 32)
            for c in range(2):
                pe.wait_ge(sem("v2_copied"), c + 1)
                pe.matmul(ps[4 + c][:, :], wgu[:, c * P:(c + 1) * P], glr[:, :], start=True, stop=True)\
                    .then_inc(sem("logit_mm"), 1)
            with pe.Fori(0, 2) as i:
                for j in range(2):
                    panel2("ccx", j, i)

            def head(h):
                return slice((h % 2) * GDK, (h % 2 + 1) * GDK), h // 2, (h % 2) * 2 + h // 2

            pe.wait_ge(bank_free, T0["mix2"] + 4)
            for h in range(GH):
                part, c, a = head(h)
                for w in range(TB):
                    ins = pe.matmul(ps[a][:, w * P:(w + 1) * P], k2[part, c, w * P:(w + 1) * P],
                                    q2[part, c, w * P:(w + 1) * P], start=True, stop=True)
                ins.then_inc(sem("self_scores"), 1)
            for lev, m in enumerate(LEVELS):
                pe.wait_ge(sem("kd_ready"), lev + 1)
                if lev:
                    pe.wait_ge(sem("lev_added"), 2 * lev)
                else:
                    pe.wait_ge(sem("logit_ready"), 2)
                for h in (0, 2, 1, 3):
                    part, c, a = head(h)
                    for w in range(TB):
                        o = c * S + w * P
                        right = qd[part, o:o + P].rearrange("p (b t) -> p b t", t=2 * m)[:, :, m:]
                        out = ps[4 + h % 2][:, (c * TB + w) * CH:(c * TB + w + 1) * CH]
                        ins = pe.matmul(out, kd[part, o:o + P], right, start=True, stop=True)
                    if c == 1:
                        ins.then_inc(sem("lev_scores"), 1)
            pe.wait_ge(sem("kd_ready"), len(LEVELS) + 1)
            for c in range(2):
                for w in range(TB):
                    ins = pe.transpose(ps[6 + c][:, w * P:(w + 1) * P], kd[:, c * S + w * P:c * S + (w + 1) * P],
                                       ident[:, :])
                ins.then_inc(sem("kdT_ready"), 1)
            pe.wait_ge(sem("kdt_copied"), 2)
            pe.wait_ge(sem("lev_added"), 2 * len(LEVELS))
            for ch in range(NCH - 1):
                w, part = ch // 2, slice((ch % 2) * CH, (ch % 2 + 1) * CH)
                if ch >= 4:
                    pe.wait_ge(sem("state_set"), ch - 3)
                for c in range(2):
                    ins = pe.matmul(ps[4 + ch % 4][:, c * 256:(c + 1) * 256], kdt[part, w, c, :],
                                    v2[part, w, c * 256:(c + 1) * 256], start=True, stop=True)
                ins.then_inc(sem("update_ready"), 1)
            pe.wait_ge(sem("state_set"), NCH - 1)
            for h in range(GH):
                part, c, a = head(h)
                for w in range(TB):
                    pe.matmul(ps[4 + h][:, w * P:(w + 1) * P], v2[:, w, h * GDV:(h + 1) * GDV],
                              at[:, a, w * P:(w + 1) * P], start=w == 0, stop=False, skip_group_check=True)
                for ch in range(1, NCH):
                    o = c * S + ch * CH
                    ins = pe.matmul(ps[4 + h][:, ch * CH:(ch + 1) * CH], state[part, c, ch, :], qe[part, o:o + CH],
                                    start=False, stop=ch == NCH - 1, skip_group_check=True)
                ins.then_inc(sem("go_ready"), 1)
            for h in range(GH):
                pe.wait_ge(sem("osq_ready"), h + 1)
                pe.matmul(ps[h][:, :], ones[:, :], osq, start=True, stop=True).then_inc(sem("go_sum"), 1)
            pe.wait_ge(sem("go_lo"), GH)
            pe.wait_ge(sem("yc_lo"), 4)
            with pe.Fori(0, 2) as i:
                for j in range(2):
                    panel2("mix2", j, i)
            ffn(2, FFN3, "up3", "dn3")

            def ple(i, j, **kw):
                n, T = N0["ple"] + j, T0["ple"] + 2 * j
                pe.wait_ge(split_done, 2 * i + (n + 1))
                tile(T, 4 * i, lambda k: slot(n, k, P), act_k, range(KD), tile_done, act_wait=kw.get("act_wait"))
                if kw.get("act_wait"):
                    sumsq(PLE)
                    pe.wait_ge(sem("p_in"), 16)
                    for c in range(2):
                        for b in range(TB):
                            ins = pe.transpose(ps[5 + c][:, b * P:(b + 1) * P], ptok[:, b, c * P:(c + 1) * P],
                                               ident[:, :])
                        ins.then_inc(sem("pf_ready"), 1)
                    pe.wait_ge(sem("pf_done"), 2)
                tile(T + 1, 4 * i, lambda k: slot(n, KD + k, P), lambda k: (pf_hi[:, k], pf_lo[:, k]), range(2),
                     panel_done)

            ple(0, 0, act_wait=f"act{PLE}")
            ple(0, 1)
            with pe.Fori(1, 4) as i:
                for j in range(2):
                    ple(i, j)
            sumsq(OUT)
            pe.wait_ge(sem("y_ready"), KD)
            pe.wait_ge(bank_free, NTILE + 4)
            for b in range(TB):
                for c in range(2):
                    if b >= 2:
                        pe.wait_ge(sem("y_copied"), 2 * b + c - 3)
                    for k in range(4):
                        ins = pe.transpose(ps[(2 * b + c) % 4][:, k * P:(k + 1) * P],
                                           x[:, 4 * c + k, b * P:(b + 1) * P], ident[:, :])
                    ins.then_inc(sem("yT_ready"), 1)

        @block.vector
        def _(ve):
            seq = Chain(ve, sem("dve_seq"))

            def lo(n, i=0):
                ve.wait_ge(hi_done, 2 * i + (n + 1))
                ve.tensor_tensor(wlo[:, n % 2], raw[:, n % 2], whi[:, n % 2].bitcast(F32), ALU.subtract)\
                    .then_inc(split_done, 1)

            def first(name, j, i=0):
                ve.wait_ge(tile_done, 2 * i + (F0[name] + j + 1))
                return bank(T0[name] + 2 * j)

            def second(name, j, i=0):
                ve.wait_ge(panel_done, 2 * i + (N0[name] + j + 1))
                return bank(T0[name] + 2 * j + 1)

            def scaled(dst, src, parts=slice(0, P)):
                ve.tensor_tensor(dst, src[parts, :], rstd[parts, :], ALU.mult).then_inc(bank_free, 1)

            def add_square(q, k, kk=None):
                ve.wait_ge(sem("sq_ready"), k + (8 * q + 1))
                if q or k:
                    ve.wait_ge(sem("sq_added"), k + 8 * q)
                ve.tensor_tensor(sqacc[:, :], sqacc[:, :], sq[:, (k if kk is None else kk) % 2], ALU.add)\
                    .then_inc(sem("sq_added"), 1)

            def gain(q, k):
                return par[:, bass.ds(NORMS[q] + k, 1)]

            def low(dst, src, high, wait, count, sig, scale=None):
                ve.wait_ge(sem(wait), count)
                if scale is None:
                    ve.tensor_tensor(dst, src, high.bitcast(F32), ALU.subtract).then_inc(sem(sig), 1)
                else:
                    ve.scalar_tensor_tensor(out=dst, in0=src, scalar=scale, in1=high.bitcast(F32), op0=ALU.mult,
                                            op1=ALU.subtract).then_inc(sem(sig), 1)

            def low_norm(q, k):
                low(act_lo[:, k], x[:, k], act_hi[:, k], f"xhi{q}", k + 1, f"act{q}", gain(q, k))

            def inv(q):
                ve.wait_ge(sem("std_ready"), q + 1)
                ve.memset(sqacc[:, :], 0.0)
                seq.link(ve.reciprocal(rstd[:, :], rstd[:, :]))

            ve.memset(eps6[:, :], 1e-6)
            ve.memset(eps5[:, :], 1e-5).then_inc(sem("consts_set"), 1)
            ve.memset(t1[:, :, :], 0.0).then_inc(bank_free, 4)
            ve.memset(t2[:, :, :], 0.0).then_inc(sem("pv_out"), 1)
            ve.memset(t3[:, :, :], 0.0).then_inc(sem("pv_ready"), 1)
            seq.link(ve.memset(sqacc[:, :], 0.0))

            for k in range(KD):
                ve.wait_ge(sem("setup_ready"), k + 1)
                ve.tensor_copy(x[:, k], ps[4 + k % 4][:, :]).then_inc(sem("setup_copied"), 1)
            ve.wait_ge(sem("setup_ready"), KD + 1)
            ve.tensor_copy(par[:, :], ps[4][:, :]).then_inc(sem("setup_copied"), 1)
            ve.wait_ge(sem("setup_copied"), KD + 1)
            lo(0)
            for k in range(KD):
                low_norm(MIX, k)
                add_square(MIX, k)

            for i in range(2):
                lo(N0["q"] + i + 1)
                if i == 0:
                    inv(MIX)
                for c in range(2):
                    src = (second if c else first)("q", i)
                    ve.scalar_tensor_tensor(out=q_sb[:, 2 * i + c], in0=src[:, :], scalar=DH ** -0.5, in1=rstd[:, :],
                                            op0=ALU.mult, op1=ALU.mult).then_inc(bank_free, 1)
            lo(N0["kvc"] + 1)
            for j in range(2):
                src = (second if j else first)("kvc", 0)
                scaled(kvc[:, j], src)
            ve.wait_ge(bank_free, T0["kvc"] + 6)

            def spread(j):
                for g in range(GR):
                    for odd in range(2):
                        ins = ve.tensor_copy(c2[odd * DH:(odd + 1) * DH, g, 0:S - odd],
                                             kvc[g * DH:(g + 1) * DH, j, odd:S])
                seq.link(ins)

            def blocks(j):
                pos = par[:, COL["cmp_pos_v" if j else "cmp_pos_k"]:][:, 0:16]
                for g in range(GR):
                    for h in range(2):
                        src = c2[:, g, 16 * h:16 * h + 16 * NCMP].rearrange("p (n l b) -> p l n b", l=8, b=2)[:, :, :, 0]
                        ins = ve.tensor_tensor(cmpf[:, 8 * h:8 * h + 8, g * NCMP:(g + 1) * NCMP], src,
                                               pos[:, 8 * h:8 * h + 8].unsqueeze(2).broadcast_to([P, 8, NCMP]),
                                               ALU.add)
                ins.then_inc(sem("cmp_set"), 1)

            spread(0)
            blocks(0)
            for br, name in enumerate(("kvs", "kvw")):
                lo(N0[name] + 1)
                scaled(k_sb[:, br], first(name, 0))
                src = second(name, 0)
                scaled(vf[:, br], src)
                ve.wait_ge(sem("vT_ready"), br + 1)
                ve.tensor_copy(v_tm[:, br, :, :].rearrange("p k c -> p (k c)"), ps[5 + br][:, :])\
                    .then_inc(sem("v_copied"), 1)
            lo(N0["gate"] + 1)
            ve.wait_ge(panel_done, N0["gate"] + 1)
            scaled(t1[0:24, 0], bank(T0["gate"]), slice(0, 24))
            lo(N0["u"] + 1)
            ve.wait_ge(sem("att_zero"), 3)
            for c in range(2):
                scaled(up[:, c, PPAD:], (second if c else first)("u", 0))
            ve.wait_ge(sem("gT_ready"), 1)
            seq.link(ve.tensor_copy(g_tm[:, :, :].rearrange("p b c -> p (b c)"), ps[7][:, 0:TB * 24]))
            lo(N0["u"] + 2)
            for c in range(2):
                scaled(up[:, 2 + c, PPAD:], (second if c else first)("u", 1))
            low(cmp_lo[:, :, :], cmpf[:, :, :], cmp_hi[:, :, :], "cmp_hi", 1, "cmp_lo")
            spread(1)
            blocks(1)
            for j, name in enumerate(("ck", "cv")):
                if j:
                    low(cmp_lo[:, :, :], cmpf[:, :, :], cmp_hi[:, :, :], "cmp_hi", 2, "cmp_lo")
                lo(N0[name] + 1)
                ve.wait_ge(panel_done, N0[name] + 1)
                ve.tensor_copy(t1[:, j, 0:62], bank(T0[name])[:, 0:62]).then_inc(bank_free, 1)
            ve.wait_ge(sem("kcmp_ready"), 1)
            for g in range(GR):
                ins = ve.tensor_copy(kbd[g * DH:(g + 1) * DH, g * NCP:g * NCP + NCMP],
                                     ps[4][0:DH, g * NCMP:(g + 1) * NCMP])
            ins.then_inc(sem("kbd_ready"), 1)
            ve.wait_ge(sem("vcmp_ready"), 1)
            for g in range(GR):
                for r in range(HPG):
                    ins = ve.tensor_copy(vbd[r * NCP:r * NCP + NCMP, g, r * DH:(r + 1) * DH],
                                         ps[5][0:NCMP, g * DH:(g + 1) * DH])
            ins.then_inc(sem("vbd_ready"), 1)
            ve.wait_ge(sem("att_consts"), 16 * 7)
            ve.wait_ge(sem("c_scores"), 1)
            cs = s_sb[:, 0, 0:1024]
            for b in range(2):
                ins = ve.tensor_tensor(s_sb[:, 0, b * S:(b + 1) * S], ps[b][:, :],
                                       cbias[:, 2 * b:2 * b + 2, :].rearrange("p b c -> p (b c)"), ALU.add)
            seq.link(ins)
            c3 = cs.rearrange("p (a n) -> p a n", n=NCP)

            def over(v):
                return v.unsqueeze(2).broadcast_to([P, 32, NCP])
            seq.link(ve.tensor_reduce(cmx[:, :], c3, AXX, ALU.max))
            ve.tensor_tensor(c3, c3, over(cmx[:, :]), ALU.subtract).then_inc(sem("c_shifted"), 1)
            ve.wait_ge(sem("c_exp"), 1)
            seq.link(ve.tensor_reduce(csm[:, :], c3, AXX, ALU.add))
            seq.link(ve.reciprocal(csm[:, :], csm[:, :]))
            for b in range(TB):
                ins = ve.tensor_tensor(csm[:, 8 * b:8 * b + 8], csm[:, 8 * b:8 * b + 8],
                                       g_tm[:, b, :].rearrange("p (h n) -> p h n", n=3)[:, :, 0], ALU.mult)
            seq.link(ins)
            seq.link(ve.tensor_tensor(c3, c3, over(csm[:, :]), ALU.mult))
            for b in range(TB):
                pb = s_sb[:, 0, b * 256:(b + 1) * 256].rearrange("p (h n) -> p h n", n=NCP)
                ins = ve.tensor_tensor(pb, pb, cvalid[:, b, :].unsqueeze(1).broadcast_to([P, 8, NCP]), ALU.mult)
            ins.then_inc(sem("c_probs"), 1)
            ve.wait_ge(sem("c_pT"), 1)
            for g in range(GR):
                ins = ve.tensor_copy(pc_t[:, g], ps[6 + g][:, :])
            ins.then_inc(sem("c_pT_copied"), 1)
            for b in (0, 2):
                ve.wait_ge(sem("c_pv"), b + 1)
                ins = ve.tensor_copy(acc[:, b], ps[b][:, :])
            ins.then_inc(sem("c_done"), 1)
            ve.wait_ge(sem("c_done"), 1)
            ve.wait_ge(sem("pt_a"), 1)

            def softmax(u, g):
                ve.wait_ge(sem("s_ready"), u + 1)
                ve.wait_ge(sem("staged"), u + 1)
                ve.memset(nmx[:, g, :], 0.0)
                for qb, bk, c in ((3, 0, 0), (2, 1, 0), (0, 1, 384), (1, 2, 0)):
                    w = (qb + 1) * P
                    ins = ve.tensor_tensor_reduce(s_sb[:, g, OFF[qb]:OFF[qb] + w], ps[3 * g + bk][:, c:c + w],
                                                  biast[:, g, S - w:S], 1.0, -3e38, ALU.add, ALU.max,
                                                  mx[:, g, qb:qb + 1])
                seq.link(ins)
                ve.tensor_scalar(nmx[:, g, :], mx[:, g, :], -1.0, None, ALU.mult).then_inc(sem("nmax_ready"), 1)

            def output(u, r, b, g):
                ve.wait_ge(sem("p_ready"), u + 1)
                seq.link(ve.reciprocal(rec[:, :], sm[:, g, :]))
                seq.link(ve.tensor_tensor(rg[:, :].unsqueeze(2), rec[:, :].unsqueeze(2),
                                          g_tm[:, :, bass.ds(3 * r + (12 * g + 1 + b), 1)], ALU.mult))
                ve.wait_ge(sem("pt_ready"), 3 * u + 2)
                ve.tensor_copy(pt[:, 512:1024], ps[7][:, :]).then_inc(sem("pt_v"), 1)
                ve.wait_ge(sem("pv_ready"), u + 2)
                seq.link(ve.tensor_tensor(otmp[:, :, :], ps[7][:, 0:TB * DH].rearrange("p (b d) -> p b d", b=TB),
                                          rg[:, :].unsqueeze(2).broadcast_to([P, TB, DH]), ALU.mult))
                o = acc[:, :, bass.ds(DH * r + g * HPG * DH, DH)]
                ve.tensor_tensor(o, o, otmp[:, :, :], ALU.add).then_inc(sem("pv_out"), 1)
                ve.wait_ge(sem("pv_out"), u + 2)

            for b in range(2):
                for g in range(GR):
                    softmax(8 * b + g, g)
                with ve.Fori(0, HPG - 1) as r:
                    seq.loop(r, 8)
                    for g in range(GR):
                        output(2 * r + (8 * b + g), r, b, g)
                        softmax(2 * r + (8 * b + g + 2), g)
                    seq.done(HPG - 1)
                for g in range(GR):
                    output(8 * b + 6 + g, HPG - 1, b, g)

            for gi in range(4):
                low(act_lo[:, 4 + gi], up[:, gi, PPAD:], act_hi[:, 4 + gi], "d_hi", gi + 1, "d_lo")
            lo(N0["pool"] + 1)
            for k in range(4):
                low(act_lo[:, k], ps[4 + k][:, :], act_hi[:, k], "o_hi", k + 1, "o_lo")
            ve.wait_ge(panel_done, N0["pool"] + 1)
            for gi in range(4):
                if gi >= 2:
                    ve.wait_ge(sem("y_hi"), gi - 1)
                ve.tensor_scalar(t1[:, gi % 2], bank(T0["pool"] + gi)[:, :],
                                 par[:, COL["pool_scale"] + gi:COL["pool_scale"] + gi + 1], None, ALU.mult)\
                    .then_inc(bank_free, 1)
                low(act_lo[:, 4 + gi], t1[:, gi % 2], act_hi[:, 4 + gi], "y_hi", gi + 1, "y_lo")

            def late(q, name, bias=None):
                for i in range(4):
                    lo(N0[name] + i + 1)
                    for c in range(2):
                        k = 2 * i + c
                        src = (second if c else first)(name, i)
                        if bias is None:
                            ve.tensor_tensor(x[:, k], x[:, k], src[:, :], ALU.add).then_inc(bank_free, 1)
                        else:
                            ve.scalar_tensor_tensor(out=x[:, k], in0=src[:, :], scalar=par[:, bias + k:bias + k + 1],
                                                    in1=x[:, k], op0=ALU.add, op1=ALU.add).then_inc(bank_free, 1)
                        add_square(q, k)
                for k in range(KD):
                    low_norm(q, k)

            late(FFN1, "mix")

            def ffn(f, q, up_, dn, qn):
                inv(q)
                with ve.Fori(0, KF // 2) as i:
                    for j in range(2):
                        lo(N0[up_] + j + 1, i)
                        scaled(t1[:, j], first(up_, j, i))
                        scaled(t2[:, j], second(up_, j, i))
                        ve.wait_ge(sem("silu_ready"), 2 * i + (KF * f + j + 1))
                        ve.wait_ge(bank_free, 4 * i + (T0[up_] + 2 * j + 6))
                        ve.tensor_tensor(t1[:, j], t2[:, j], t3[:, j], ALU.mult).then_inc(sem("hidden_set"), 1)
                        k = bass.ds(2 * i + j, 1)
                        ve.wait_ge(sem("hidden_hi"), 2 * i + (KF * f + j + 1))
                        ve.tensor_tensor(hid_lo[:, k, :], t1[:, j], hid_hi[:, k, :].bitcast(F32), ALU.subtract)\
                            .then_inc(sem("hidden_lo"), 1)
                if qn == FINAL:
                    ve.wait_ge(sem("hidden_lo"), KF * (f + 1))
                with ve.Fori(0, 2) as i:
                    for j in range(4):
                        lo(N0[dn] + 2 * j + 1, 4 * i)
                        lo(N0[dn] + 2 * j + 2, 4 * i)
                        ve.wait_ge(panel_done, 8 * i + (N0[dn] + 2 * j + 2))
                        k = 4 * i + j
                        xk = x[:, bass.ds(k, 1), :]
                        ve.tensor_tensor(xk, xk, bank(T0[dn] + j)[:, :], ALU.add).then_inc(bank_free, 1)
                        add_square(qn, k, j)
                        if qn != FINAL:
                            kk = bass.ds(k, 1)
                            low(act_lo[:, kk, :], xk, act_hi[:, kk, :], f"xhi{qn}", k + 1, f"act{qn}", gain(qn, k))

            ffn(0, FFN1, "up1", "dn1", CONVIN)

            ve.memset(z[:, :, 0:CPAD], 0.0)
            inv(CONVIN)
            taps_of = par[:, P:P + CONV * KD].rearrange("p (t m) -> p t m", m=KD)
            with ve.Fori(0, 4) as i:
                seq.loop(i, 2 * CONV)
                for j in range(2):
                    m = 2 * i + j
                    lo(N0["pw1"] + j + 1, i)
                    seq.link(ve.tensor_copy(wtap[:, j].unsqueeze(2), taps_of[:, :, bass.ds(m, 1)]))
                    scaled(t1[:, j], first("pw1", j, i))
                    scaled(t2[:, j], second("pw1", j, i))
                    ve.wait_ge(sem("glu_sig"), 2 * i + (j + 1))
                    ve.scalar_tensor_tensor(out=z[:, j, CPAD:], in0=t1[:, j],
                                            scalar=par[:, bass.ds(2 * i + (COL["conv_b_pw1"] + j), 1)],
                                            in1=t3[:, j], op0=ALU.add, op1=ALU.mult).then_inc(sem("z_ready"), 1)
                    ve.wait_ge(sem("z_ready"), 2 * i + (j + 1))
                    seq.link(ve.tensor_scalar(t2[:, j], z[:, j, 0:S], wtap[:, j, 0:1],
                                              par[:, bass.ds(2 * i + (COL["conv_b_dw"] + j), 1)], ALU.mult, ALU.add))
                    for tap in range(1, CONV):
                        last = tap == CONV - 1
                        dst = zc[:, bass.ds(m, 1), :] if last else t2[:, j]
                        ins = ve.scalar_tensor_tensor(out=dst, in0=z[:, j, tap:tap + S], scalar=wtap[:, j, tap:tap + 1],
                                                      in1=t2[:, j], op0=ALU.mult, op1=ALU.add)
                        if last:
                            ins.then_inc(sem("zc_ready"), 1)
                        else:
                            seq.link(ins)
                seq.done(4)
            ve.wait_ge(sem("zc_ready"), KD)
            seq.link(ve.tensor_tensor(zsum[:, :], zc[:, 0], zc[:, 1], ALU.add))
            for k in range(2, KD):
                ins = ve.tensor_tensor(zsum[:, :], zsum[:, :], zc[:, k], ALU.add)
                if k < KD - 1:
                    seq.link(ins)
            ins.then_inc(sem("zsum_ready"), 1)
            ve.wait_ge(sem("zmean_ready"), 1)
            seq.link(ve.tensor_scalar(mean[:, :], ps[5][:, :], 1.0 / D, None, ALU.mult))
            for k in range(KD):
                ve.tensor_tensor(zc[:, k], zc[:, k], mean[:, :], ALU.subtract).then_inc(sem("ln_centered"), 1)
                if k:
                    add_square(LN, k - 1)
            add_square(LN, KD - 1)
            inv(LN)
            for k in range(KD + 1):
                if k < KD:
                    if k >= 2:
                        ve.wait_ge(sem("zhi"), k - 1)
                    ve.wait_ge(sem("ln_centered"), k + 1)
                    ve.tensor_tensor(t1[:, k % 2], zc[:, k], rstd[:, :], ALU.mult).then_inc(sem("ln_scaled"), 1)
                if k:
                    low(act_lo[:, k - 1], t3[:, (k - 1) % 2], act_hi[:, k - 1], "zhi", k, "zlo")
            late(FFN2, "pw2", COL["conv_b_pw2"])
            ffn(1, FFN2, "up2", "dn2", FINAL)

            inv(FINAL)
            for k in range(KD):
                ve.scalar_tensor_tensor(out=x[:, k], in0=x[:, k], scalar=gain(FINAL, k), in1=rstd[:, :],
                                        op0=ALU.mult, op1=ALU.mult).then_inc(sem("x_final"), 1)
                if k:
                    low_norm(GLAIN, k - 1)
                    add_square(GLAIN, k - 1)
            low_norm(GLAIN, KD - 1)
            add_square(GLAIN, KD - 1)

            for i, dst in enumerate((q2, k2)):
                lo(N0["qk2"] + i + 1)
                if i == 0:
                    inv(GLAIN)
                for c in range(2):
                    src = (second if c else first)("qk2", i)
                    ve.scalar_tensor_tensor(out=dst[:, c], in0=src[:, :], scalar=1.0 if i else GDK ** -0.5,
                                            in1=rstd[:, :], op0=ALU.mult, op1=ALU.mult).then_inc(bank_free, 1)
            for name, dst in (("v2", v2f), ("g2", gs)):
                for i in range(2):
                    lo(N0[name] + i + 1)
                    for c in range(2):
                        scaled(dst[:, 2 * i + c], (second if c else first)(name, i))
            lo(N0["glr"] + 1)
            ve.wait_ge(panel_done, N0["glr"] + 1)
            scaled(glr[:, :], bank(T0["glr"]), slice(0, 16))
            for w in range(TB):
                ve.wait_ge(sem("v2T_ready"), w + 1)
                ve.tensor_copy(v2[:, w], ps[4 + w][:, :]).then_inc(sem("v2_copied"), 1)
            for i in range(2):
                lo(N0["cb2"] + i + 1)
                for c in range(2):
                    scaled(cbt[:, 2 * i + c], (second if c else first)("cb2", i))
            for c in range(2):
                ve.wait_ge(sem("logit_mm"), c + 1)
                ve.tensor_scalar(la[:, c * S:(c + 1) * S], ps[4 + c][:, :],
                                 par[:, COL["b_gate_2"] + c:COL["b_gate_2"] + c + 1], None, ALU.add)\
                    .then_inc(sem("logit_ready"), 1)
            ve.wait_ge(sem("gla_set"), 3)
            for i in range(4):
                lo(N0["ccx"] + i + 1)
                scaled(t1[:, i % 2], first("ccx", i))
                scaled(t2[:, i % 2], second("ccx", i))
                ve.wait_ge(bank_free, T0["ccx"] + 2 * i + 6)
                seq.link(ve.tensor_tensor(ccx[:, i, 2:], t1[:, i % 2], t2[:, i % 2], ALU.mult))
            ve.wait_ge(sem("softplus_ready"), 1)
            seq.link(ve.scalar_tensor_tensor(out=la[:, :], in0=la[:, :], scalar=0.0, in1=la2[:, :], op0=ALU.min,
                                             op1=ALU.subtract))
            seq.link(ve.tensor_tensor_scan(bc[:, :], scan1[:, :], la[:, :], 0.0, ALU.mult, ALU.add))
            seq.link(ve.tensor_scalar(bc[:, :], bc[:, :], 1.0 / 16.0, None, ALU.mult))
            for a in range(GH):
                ve.wait_ge(sem("self_scores"), (1, 3, 2, 4)[a])
                ve.tensor_tensor(at[:, a].rearrange("p (w t) -> p w t", w=TB),
                                 ps[a][:, :].rearrange("p (w t) -> p w t", w=TB),
                                 ident[:, :].unsqueeze(1).broadcast_to([P, TB, P]), ALU.mult)
            q2f, k2f = (v[:, :, :].rearrange("p c t -> p (c t)") for v in (q2, k2))
            for lev, m in enumerate(LEVELS):
                b3 = bc[:, :].rearrange("p (b t) -> p b t", t=2 * m)
                if lev:
                    ve.wait_ge(sem("ex_ready"), lev)
                ve.tensor_tensor(dd[:, :].rearrange("p (b t) -> p b t", t=2 * m), b3,
                                 b3[:, :, m - 1:m].broadcast_to([P, 2 * S // (2 * m), 2 * m]), ALU.subtract)\
                    .then_inc(sem("dd_ready"), 1)
                ve.wait_ge(sem("ex_ready"), lev + 1)
                if lev:
                    ve.wait_ge(sem("lev_scores"), 2 * lev)
                ve.tensor_tensor(qd[:, :], q2f, ex[:, :], ALU.mult)
                ve.tensor_tensor(kd[:, :], k2f, ex[:, :], ALU.mult).then_inc(sem("kd_ready"), 1)
                for h in range(2):
                    ve.wait_ge(sem("lev_scores"), 2 * lev + h + 1)
                    tmp = t1[:, h, :]
                    seq.link(ve.tensor_tensor(tmp.rearrange("p (a c) -> p a c", c=CH),
                                              ps[4 + h][:, :].rearrange("p (a c) -> p a c", c=CH),
                                              glm[:, lev, :].unsqueeze(1).broadcast_to([P, 2 * TB, CH]), ALU.mult))
                    dst = at[:, 2 * h:2 * h + 2].rearrange("p a t -> p (a t)").rearrange(
                        "p (b t) -> p b t", t=2 * m)[:, :, m:]
                    ve.tensor_tensor(dst, dst, tmp.rearrange("p (b t) -> p b t", t=m), ALU.add)\
                        .then_inc(sem("lev_added"), 1)
                    ve.wait_ge(sem("lev_added"), 2 * lev + h + 1)
            c3 = bc[:, :].rearrange("p (c t) -> p c t", t=CH)
            ve.tensor_tensor(dd[:, :].rearrange("p (c t) -> p c t", t=CH),
                             c3[:, :, CH - 1:CH].broadcast_to([P, 2 * NCH, CH]), c3, ALU.subtract)\
                .then_inc(sem("dd_ready"), 1)
            ve.wait_ge(sem("ex_ready"), len(LEVELS) + 1)
            ve.tensor_tensor(kd[:, :], k2f, ex[:, :], ALU.mult).then_inc(sem("kd_ready"), 1)
            ve.wait_ge(sem("ebc_ready"), 1)
            seq.link(ve.tensor_tensor(qe[:, :], q2f, la2[:, :], ALU.mult))
            for c in range(2):
                ve.wait_ge(sem("kdT_ready"), c + 1)
                ve.tensor_copy(kdt[:, :, c, :], ps[6 + c][:, :].rearrange("p (w n) -> p w n", w=TB))\
                    .then_inc(sem("kdt_copied"), 1)
            for ch in range(NCH - 1):
                ve.wait_ge(sem("update_ready"), ch + 1)
                if ch:
                    ve.wait_ge(sem("state_set"), ch)
                for h in range(2):
                    for c in range(2):
                        part = slice(h * GDK, (h + 1) * GDK)
                        up_ps = ps[4 + ch % 4][part, c * 256 + h * GDV:c * 256 + (h + 1) * GDV]
                        e = c * S + ch * CH + CH - 1
                        if ch == 0:
                            ins = ve.tensor_copy(state[part, c, 1, :], up_ps)
                        else:
                            ins = ve.scalar_tensor_tensor(out=state[part, c, ch + 1, :], in0=state[part, c, ch, :],
                                                          scalar=la2[part, e:e + 1], in1=up_ps, op0=ALU.mult,
                                                          op1=ALU.add)
                ins.then_inc(sem("state_set"), 1)
            for k in range(4):
                w3 = [par[:, COL["conv_w_2"] + tap * 4 + k:COL["conv_w_2"] + tap * 4 + k + 1] for tap in range(3)]
                seq.link(ve.tensor_scalar(t2[:, k % 2], ccx[:, k, 0:S], w3[0], None, ALU.mult))
                for tap in (1, 2):
                    seq.link(ve.scalar_tensor_tensor(out=t2[:, k % 2], in0=ccx[:, k, tap:tap + S], scalar=w3[tap],
                                                     in1=t2[:, k % 2], op0=ALU.mult, op1=ALU.add))
                ve.tensor_tensor(cbt[:, k], cbt[:, k], t2[:, k % 2], ALU.mult).then_inc(sem("yc_ready"), 1)
            for h in range(GH):
                ve.wait_ge(sem("go_std"), h + 1)
                ve.reciprocal(rstd[:, :], t3[:, h % 2]).then_inc(sem("go_rstd"), 1)
                ve.wait_ge(sem("go_rstd"), h + 1)
                seq.link(ve.tensor_tensor(t2[:, h % 2], ps[4 + h][:, :], rstd[:, :], ALU.mult))
                if h == 0:
                    ve.wait_ge(sem("gs_ready"), GH)
                ve.scalar_tensor_tensor(out=t1[:, h % 2], in0=t2[:, h % 2], scalar=par[:, COL["gn_g_2"]:COL["gn_g_2"] + 1],
                                        in1=gs[:, h], op0=ALU.mult, op1=ALU.mult).then_inc(sem("go_out"), 1)
                low(act_lo[:, h], t1[:, h % 2], act_hi[:, h], "go_hi", h + 1, "go_lo")
            for k in range(4):
                low(act_lo[:, 4 + k], cbt[:, k], act_hi[:, 4 + k], "yc_hi", k + 1, "yc_lo")
            late(FFN3, "mix2")
            ffn(2, FFN3, "up3", "dn3", PLE)

            inv(PLE)
            for c in range(2):
                low(pf_lo[:, c], ps[5 + c][:, :], pf_hi[:, c], "pf_hi", c + 1, "pf_done")

            def ple(i, j, more):
                if more:
                    lo(N0["ple"] + j + 1, i)
                scaled(t1[:, j], first("ple", j, i))
                src = second("ple", j, i)
                ve.wait_ge(sem("ple_sig"), 2 * i + (j + 1))
                ve.tensor_tensor(t2[:, j], src[:, :], t3[:, j], ALU.mult).then_inc(bank_free, 1)
                ve.wait_ge(bank_free, 4 * i + (T0["ple"] + 2 * j + 6))
                xk = x[:, bass.ds(2 * i + j, 1), :]
                ve.tensor_tensor(xk, xk, t2[:, j], ALU.add).then_inc(sem("ple_x"), 1)
                add_square(OUT, 2 * i + j, j)

            with ve.Fori(0, 3) as i:
                for j in range(2):
                    ple(i, j, True)
            ple(3, 0, True)
            ple(3, 1, False)
            inv(OUT)
            for k in range(KD):
                ve.scalar_tensor_tensor(out=x[:, k], in0=x[:, k], scalar=gain(OUT, k), in1=rstd[:, :],
                                        op0=ALU.mult, op1=ALU.mult).then_inc(sem("y_ready"), 1)
            for b in range(TB):
                for c in range(2):
                    ve.wait_ge(sem("yT_ready"), 2 * b + c + 1)
                    ve.tensor_copy(yt[:, b, c * S:(c + 1) * S], ps[(2 * b + c) % 4][:, :]).then_inc(sem("y_copied"), 1)


_CONSTS = ["ident", "dist", "slopes", "cbias", "cvalid", "pinv", "glm"]
_INS = ["x", "mix_norm", "ffn_norm", "nsa_w_in", "cmp_pos_k", "cmp_pos_v", "cmp_k_w1", "cmp_k_w2", "cmp_v_w1",
        "cmp_v_w2", "pool_w", "pool_scale", "mix_w_out", "conv_w_pw1", "conv_b_pw1", "conv_w_dw", "conv_b_dw",
        "conv_ln_g", "conv_ln_b", "conv_w_pw2", "conv_b_pw2", "ffn_w_gate", "ffn_w_up", "ffn_w_down", "final_norm",
        "p_2", "ln1_g_2", "w_in_2", "w_gate_up_2", "b_gate_2", "conv_w_2", "gn_g_2", "w_out_2", "ln2_g_2",
        "w_gate_upffn_2", "w_down_2", "ln3_g_2", "w_ple_gate_2", "w_ple_proj_2", "lnf_g_2"]


def constants():
    import numpy as np
    f = np.float32
    p, c = np.arange(P)[:, None], np.arange(S)[None, :]
    d = p - c + (S - P)
    slope = 2.0 ** (-8.0 * np.arange(1, NH + 1) / NH)
    tok = np.arange(P)[:, None, None] + P * np.arange(TB)[None, :, None]
    end = np.arange(NCP)[None, None, :] * 16 + 31
    cd = tok - end
    valid = (cd >= 0) & (np.arange(NCP)[None, None, :] < NCMP)
    cb = np.where(valid[:, :, None, :], -slope[None, None, :, None] * cd[:, :, None, :], -1e30)
    glm = np.zeros((P, len(LEVELS), CH), f)
    for lev, m in enumerate(LEVELS):
        t = np.arange(CH)
        blk = t // m
        glm[:, lev] = (np.arange(P)[:, None] // m == 2 * blk[None, :])
    return {
        "ident": np.eye(P, dtype=f),
        "dist": np.where(d >= 0, d, 1e30).astype(f),
        "slopes": np.broadcast_to(-slope, (P, NH)).astype(f),
        "cbias": cb.reshape(P, TB, 256).astype(f),
        "cvalid": valid.astype(f),
        "pinv": np.broadcast_to(1.0 / np.arange(1, PPAD + 1), (P, PPAD)).astype(f),
        "glm": glm,
    }


def kernel(**inputs):
    import numpy as _np
    import concourse.bacc as _bacc
    from concourse.bass_utils import run_bass_kernel_spmd as _run

    nc = _bacc.Bacc("TRN2", target_bir_lowering=False, num_devices=1)
    arrays, tensors = {}, {}
    consts = constants()
    for name in _INS + _CONSTS:
        a = _np.ascontiguousarray(consts[name] if name in consts else inputs[name])
        arrays[f"in_{name}_dram"] = a
        tensors[name] = nc.dram_tensor(f"in_{name}_dram", a.shape, mybir.dt.from_np(a.dtype), kind="ExternalInput").ap()
    tensors["out"] = nc.dram_tensor("out_0_dram", (1, S, D), F32, kind="ExternalOutput").ap()
    program(nc, tensors)
    r = _run(nc, [arrays], core_ids=[0])
    return r.results[0]["out_0_dram"]
```

```python
from contextlib import ExitStack

import concourse.bass as bass
from concourse import mybir

F32 = mybir.dt.float32
F32R = mybir.dt.float32r
ALU = mybir.AluOpType
ACT = mybir.ActivationFunctionType
AXX = mybir.AxisListType.X

P = 128
S = 512
TB = S // P
D = 1024
KD = D // P
SLOT = 2048
NH, GR, HPG, DH = 8, 2, 4, 64
NCMP = 31
NCP = 32
FH = 2816
KF = FH // P
KHALF = KF // 2
IN1 = 1816
CONV = 31
CPAD = CONV - 1
PETAPS = 12
PPAD = 16
CH = 64
NCH = S // CH
GH, GDK, GDV = 4, 64, 128
LEVELS = (32, 16, 8, 4, 2, 1)

PHASES = [
    ("q", 2, 2), ("kvc", 1, 2), ("gate", 1, 1), ("u", 2, 2),
    ("ck", 1, 1), ("cv", 1, 1), ("kvs", 1, 2), ("kvw", 1, 2), ("pool", 1, 4), ("mix", 4, 2),
    ("up1", KF, 2), ("dn1", 16, 0.5), ("pw1", 8, 2), ("pw2", 4, 2), ("up2", KF, 2), ("dn2", 16, 0.5),
    ("glr", 1, 1), ("qk2", 2, 2), ("v2", 2, 2), ("cb2", 2, 2), ("ccx", 4, 2), ("g2", 2, 2), ("mix2", 4, 2),
    ("up3", KF, 2), ("dn3", 16, 0.5), ("ple", 8, 2),
]
N0, T0, F0 = {}, {}, {}
_n = _t = _f = 0
for _name, _c, _per in PHASES:
    N0[_name], T0[_name], F0[_name] = _n, _t, _f
    _n, _t = _n + _c, _t + int(_c * _per)
    _f += _c if _per == 2 else 0
NPANEL, NTILE = _n, _t

PARAMS = [("mix_norm", 16), ("ffn_norm", 16), ("final_norm", 8), ("ln1_g_2", 8), ("ln2_g_2", 8), ("ln3_g_2", 8),
          ("lnf_g_2", 8), ("pool_scale", 4), ("conv_b_pw1", 16), ("conv_b_dw", 8), ("conv_ln_g", 8),
          ("conv_ln_b", 8), ("conv_b_pw2", 8), ("b_gate_2", 2), ("gn_g_2", 1)]
COL = {}
_c = 0
for _name, _k in PARAMS:
    COL[_name] = _c
    _c += _k
COL["conv_w_dw"] = P
COL["conv_w_2"] = 3 * P
COL["cmp_pos_k"] = 3 * P + 32
COL["cmp_pos_v"] = 3 * P + 64

NORMS = [COL["mix_norm"], COL["ffn_norm"], COL["mix_norm"] + 8, COL["ffn_norm"] + 8, COL["final_norm"],
         COL["ln1_g_2"], COL["ln2_g_2"], COL["ln3_g_2"], COL["lnf_g_2"]]
NORMS.insert(3, None)
MIX, FFN1, CONVIN, LN, FFN2, FINAL, GLAIN, FFN3, PLE, OUT = range(10)
OFF = {3: 0, 2: 512, 0: 896, 1: 1024}


class Chain:

    def __init__(self, eng, sem):
        self.eng, self.sem, self.base, self.j = eng, sem, 0, 0

    def link(self, ins, behind=0):
        ins.then_inc(self.sem, 1)
        self.j += 1
        self.eng.wait_ge(self.sem, self.base + (self.j - behind))

    def loop(self, i, per, first=0):
        self.before = self.base + self.j
        self.base, self.j, self.per = i * per + (self.before - first * per), 0, per

    def done(self, count):
        assert self.j == self.per, self.j
        self.base, self.j = self.before + count * self.per, 0


def program(nc, t):
    ctx = ExitStack()
    with ctx:
        def sb(name, shape, dt=F32):
            return ctx.enter_context(nc.sbuf_tensor(name, shape, dt))

        sems = {}

        def sem(name):
            if name not in sems:
                sems[name] = ctx.enter_context(nc.semaphore(name))
            return sems[name]

        raw = sb("raw", [P, 2, SLOT])
        whi = sb("whi", [P, 2, SLOT], F32R)
        wlo = sb("wlo", [P, 2, SLOT], F32R)
        x = sb("x", [P, KD, S])
        act_hi = sb("act_hi", [P, KD, S], F32R)
        act_lo = sb("act_lo", [P, KD, S], F32R)
        rstd = sb("rstd", [P, S])
        sq = sb("sq", [P, 2, S])
        sqacc = sb("sqacc", [P, S])
        ones = sb("ones", [P, P])
        ident = sb("ident", [P, P])
        par = sb("par", [P, 4 * P])
        eps6 = sb("eps6", [P, 1])
        eps5 = sb("eps5", [P, 1])
        t1 = sb("t1", [P, 2, S])
        t2 = sb("t2", [P, 2, S])
        t3 = sb("t3", [P, 2, S])
        wtap = sb("wtap", [P, 2, CONV])

        tok_rstd = wtap[:, 1, 0:TB]

        def region(parts):
            got = []
            with ExitStack() as r:
                for name, shape, dt in parts:
                    got.append(r.enter_context(nc.sbuf_tensor(name, shape, dt)))
            return got

        xt, prow = region([("xt", [P, TB, D], F32), ("prow", [P, 4, P], F32)])
        (q_hi, q_lo, k_hi, k_lo, vf, v_tm, cmp_hi, cmp_lo, g_tm, kbd, kbd_hi, kbd_lo, vbd, ghid, w2c, cvalid, pinv, up,
         wsum, dist, slopes, slope_st, biast, s_sb, pt, acc, mx, nmx, sm, rec, rg, otmp, cmx, csm,
         ) = region([
             ("q_hi", [P, HPG, S], F32R), ("q_lo", [P, HPG, S], F32R), ("k_hi", [P, 2, S], F32R),
             ("k_lo", [P, 2, S], F32R), ("vf", [P, 2, S], F32),
             ("v_tm", [P, 2, TB, P], F32), ("cmp_hi", [P, 16, 62], F32R), ("cmp_lo", [P, 16, 62], F32R),
             ("g_tm", [P, TB, 24], F32), ("kbd", [P, 2 * NCP], F32), ("kbd_hi", [P, 2 * NCP], F32R),
             ("kbd_lo", [P, 2 * NCP], F32R), ("vbd", [P, GR, HPG * DH], F32),
             ("ghid", [P, 2, 62], F32), ("w2c", [P, 2, DH], F32), ("cvalid", [P, TB, NCP], F32), ("pinv", [P, PPAD], F32), ("up", [P, 4, PPAD + S], F32),
             ("wsum", [P, 2, PPAD + S], F32), ("dist", [P, S], F32), ("slopes", [P, NH], F32), ("slope_st", [P, GR], F32),
             ("biast", [P, 2, S], F32), ("s_sb", [P, 2, 1280], F32),
             ("pt", [P, 1280], F32), ("acc", [P, TB, NH * DH], F32), ("mx", [P, 2, TB], F32),
             ("nmx", [P, 2, TB], F32), ("sm", [P, 2, TB], F32), ("rec", [P, TB], F32), ("rg", [P, TB], F32),
             ("otmp", [P, TB, DH], F32), ("cmx", [P, 32], F32), ("csm", [P, 32], F32),
         ])
        q_st = [v[:, :, :].rearrange("p k n -> p (k n)")[:, 0:S] for v in (cmp_hi, cmp_lo)]
        gsig = t2[0:24, 0]
        cbias = s_sb[:, 1, 0:TB * 256].rearrange("p (b c) -> p b c", b=TB)
        c2 = acc[:, 0:2, :]
        cmpf = acc[:, 2:4, :].rearrange("p b c -> p (b c)")[:, 0:16 * 62].rearrange("p (k n) -> p k n", k=16)
        y_f = [t1[:, 0], t1[:, 1], t3[:, 0], t3[:, 1]]
        q_f, k_f = up[:, :, PPAD:], t2
        kvc = pc_t = pt[:, 0:2 * S].rearrange("p (j t) -> p j t", j=2)
        hid_hi, hid_lo = region([("hid_hi", [P, KF, S], F32R), ("hid_lo", [P, KF, S], F32R)])
        z, zc, mean, zsum, z_hi, z_lo, tap_hi, tap_lo, diag_hi, diag_lo = region([
            ("z", [P, 2, CPAD + S], F32), ("zc", [P, KD, S], F32), ("mean", [P, S], F32), ("zsum", [P, S], F32),
            ("z_hi", [P, 2, CPAD + S], F32R), ("z_lo", [P, 2, CPAD + S], F32R),
            ("tap_hi", [P, CONV * KD], F32R), ("tap_lo", [P, CONV * KD], F32R),
            ("diag_hi", [P, 2, PETAPS, P], F32R), ("diag_lo", [P, 2, PETAPS, P], F32R),
        ])
        (q2, k2, v2f, v2, gs, cbt, ccx, at, glr, wgu, la, la2, scan1, bc, qkd, glm, kdt, qe) = region([
            ("q2", [P, 2, S], F32), ("k2", [P, 2, S], F32), ("v2f", [P, GH, S], F32),
            ("v2", [P, TB, GH * GDV], F32), ("gs", [P, GH, S], F32), ("cbt", [P, 4, S], F32),
            ("ccx", [P, 2, 2 + S], F32), ("at", [P, GH, S], F32), ("glr", [16, S], F32), ("wgu", [16, 256], F32),
            ("la", [P, 2 * S], F32), ("la2", [P, 2 * S], F32), ("scan1", [P, 2 * S], F32),
            ("bc", [P, 2 * S], F32), ("qkd", [P, 2, 2 * S], F32), ("glm", [P, len(LEVELS), CH], F32),
            ("kdt", [P, TB, 2, P], F32), ("qe", [P, 2 * S], F32),
        ])
        dd, ex, gla_o = la, scan1, v2f
        head_rstd = wtap[:, 0, 0:GH * TB]
        osq = [sq[:, 0], sq[:, 1], dd[:, 0:S], dd[:, S:]]
        qd, kd = qkd[:, 0], qkd[:, 1]
        state = qkd[:, :, :].rearrange("p c (n v) -> p c n v", v=GDV)
        yt, ptok, pf_hi, pf_lo = region([("yt", [P, TB, D], F32), ("ptok", [P, TB, 256], F32),
                                         ("pf_hi", [P, 2, S], F32R), ("pf_lo", [P, 2, S], F32R)])

        ps = [ctx.enter_context(nc.psum_tensor(f"ps{i}", [P, S], F32)) for i in range(8)]

        raw_full = [sem("raw_full0"), sem("raw_full1")]
        hi_done, split_done = sem("hi_done"), sem("split_done")
        panel_done, tile_done, bank_free = sem("panel_done"), sem("tile_done"), sem("bank_free")

        def bank(tile):
            return ps[tile % 4]

        block = ctx.enter_context(nc.Block())

        @block.sync
        def _(sp):
            def load(n, slot, halves):
                if not (isinstance(n, int) and n < 2):
                    sp.wait_ge(split_done, n - 1)
                for dst, src in halves:
                    sp.dma_start(dst, src).then_inc(raw_full[slot], 16)

            def slot8(s):
                return raw[:, s].rearrange("p (k j c) -> p k j c", k=KD, j=2)

            def cols256(w, c0, s):
                v = w.rearrange("(k p) n -> p k n", p=P)
                r = raw[:, s].rearrange("p (k c) -> p k c", k=KD)
                return [(r[:, 0:4, :], v[:, 0:4, c0]), (r[:, 4:8, :], v[:, 4:8, c0])]

            def pair(w, c0, c1, s):
                v = w.rearrange("(k p) n -> p k n", p=P)
                r = slot8(s)
                return [(r[:, :, 0, :], v[:, :, c0]), (r[:, :, 1, :], v[:, :, c1])]

            def straight(name, count, halves):
                for i in range(count):
                    n = N0[name] + i
                    load(n, n % 2, halves(i, n % 2))

            def looped(name, count, halves):
                with sp.Fori(0, count // 2) as i:
                    for j in range(2):
                        n = N0[name] + j
                        load(2 * i + n, n % 2, halves(2 * i + j, n % 2))

            sp.dma_start(ident[:, :], t["ident"]).then_inc(sem("ident_in"), 16)
            for b in range(TB):
                sp.dma_start(xt[:, b, :], t["x"][0, b * P:(b + 1) * P, :]).then_inc(sem("x_in"), 16)
            sp.wait_ge(sem("prow_zero"), 1)
            taps = t["conv_w_dw"][0].rearrange("j (m c) -> (j m) c", c=P)
            sp.dma_start(prow[:, 1, :], taps[0:P]).then_inc(sem("taps_in"), 16)
            sp.dma_start(prow[0:CONV * KD - P, 2, :], taps[P:CONV * KD]).then_inc(sem("taps_in"), 16)
            sp.dma_start(prow[0:12, 3, :], t["conv_w_2"][0].rearrange("j (m c) -> (j m) c", c=P))\
                .then_inc(sem("taps_in"), 16)
            for name, row in (("cmp_pos_k", 32), ("cmp_pos_v", 64)):
                sp.dma_start(prow[row:row + 16, 3, :], t[name][0].rearrange("(j b) c -> j (b c)", b=2))\
                    .then_inc(sem("taps_in"), 16)
            w = t["nsa_w_in"][0]
            straight("q", 2, lambda i, s: [
                (raw[:, s].rearrange("p (k r g c) -> p k r g c", k=KD, r=2, g=2)[:, :, r, g, :],
                 w.rearrange("(k p) n -> p k n", p=P)[:, :, (g * HPG + 2 * i + r) * DH:(g * HPG + 2 * i + r + 1) * DH])
                for r in range(2) for g in range(2)])
            straight("kvc", 1, lambda i, s: cols256(w, bass.ds(512, 256), s))
            straight("gate", 1, lambda i, s: [
                (slot8(s)[:, a:a + 4, 0, 0:24], w.rearrange("(k p) n -> p k n", p=P)[:, a:a + 4, 1280:1304])
                for a in (0, 4)])
            straight("u", 2, lambda i, s: cols256(w, bass.ds(1304 + 256 * i, 256), s))
            for name in ("ck", "cv"):
                w1 = t["cmp_k_w1" if name == "ck" else "cmp_v_w1"][0].rearrange("(k p) n -> p k n", p=P)
                straight(name, 1, lambda i, s: [
                    (raw[:, s].rearrange("p (k c) -> p k c", c=P)[:, a:a + 8], w1[:, a:a + 8]) for a in (0, 8)])
            for j, name in enumerate(("kvs", "kvw")):
                straight(name, 1, lambda i, s: cols256(w, bass.ds(768 + 256 * j, 256), s))
            straight("pool", 1, lambda i, s: [
                (raw[:, s, 0:512].rearrange("p (g e) -> p g e", g=4)[:, a:a + 2],
                 t["pool_w"][0].rearrange("g c e -> c g e")[:, a:a + 2]) for a in (0, 2)])
            looped("mix", 4, lambda i, s: cols256(t["mix_w_out"][0], bass.ds(i * 256, 256), s))

            def ffn(up, dn, wg, wu, wd, off):
                looped(up, KF, lambda i, s: pair2(wg, bass.ds(i * 128, 128), wu, bass.ds(off + i * 128, 128), s))
                wdv = wd.rearrange("(h k p) n -> p h k n", p=P, h=2)
                r = [raw[:, s, 0:KHALF * P].rearrange("p (k c) -> p k c", k=KHALF) for s in range(2)]
                n = N0[dn]
                with sp.Fori(0, KD) as m:
                    for h in range(2):
                        s = (n + h) % 2
                        load(2 * m + n + h, s, [
                            (r[s][:, 0:6, :], wdv[:, h, 0:6, bass.ds(m * P, P)]),
                            (r[s][:, 6:KHALF, :], wdv[:, h, 6:KHALF, bass.ds(m * P, P)])])

            def pair2(wa, c0, wb, c1, s):
                r = slot8(s)
                return [(r[:, :, 0, :], wa.rearrange("(k p) n -> p k n", p=P)[:, :, c0]),
                        (r[:, :, 1, :], wb.rearrange("(k p) n -> p k n", p=P)[:, :, c1])]

            ffn("up1", "dn1", t["ffn_w_gate"][0], t["ffn_w_up"][0], t["ffn_w_down"][0], 0)
            w = t["conv_w_pw1"][0]
            looped("pw1", 8, lambda i, s: pair(w, bass.ds(i * 128, 128), bass.ds(i * 128 + D, 128), s))
            looped("pw2", 4, lambda i, s: cols256(t["conv_w_pw2"][0], bass.ds(i * 256, 256), s))
            ffn("up2", "dn2", t["ffn_w_gate"][1], t["ffn_w_up"][1], t["ffn_w_down"][1], 0)
            w2 = t["w_in_2"][0]
            straight("glr", 1, lambda i, s: [
                (slot8(s)[:, a:a + 4, 0, 0:16], w2.rearrange("(k p) n -> p k n", p=P)[:, a:a + 4, 1536:1552])
                for a in (0, 4)])
            straight("qk2", 2, lambda i, s: cols256(w2, bass.ds(256 * i, 256), s))
            straight("v2", 2, lambda i, s: cols256(w2, bass.ds(512 + 256 * i, 256), s))
            straight("cb2", 2, lambda i, s: cols256(w2, bass.ds(1552 + 256 * i, 256), s))
            looped("ccx", 4, lambda i, s: pair(w2, bass.ds(i * 128 + 2064, 128), bass.ds(i * 128 + 2576, 128), s))
            straight("g2", 2, lambda i, s: cols256(w2, bass.ds(1024 + 256 * i, 256), s))
            looped("mix2", 4, lambda i, s: cols256(t["w_out_2"][0], bass.ds(i * 256, 256), s))
            ffn("up3", "dn3", t["w_gate_upffn_2"][0], t["w_gate_upffn_2"][0], t["w_down_2"][0], FH)

            def ple(i, s):
                r = raw[:, s, 0:1280].rearrange("p (k c) -> p k c", c=P)
                return [(r[:, 0:8], t["w_ple_gate_2"][0].rearrange("(k p) n -> p k n", p=P)[:, :, bass.ds(i * P, P)]),
                        (r[:, 8:10], t["w_ple_proj_2"][0].rearrange("(k p) n -> p k n", p=P)[:, :, bass.ds(i * P, P)])]
            looped("ple", 8, ple)
            for b in range(TB):
                sp.wait_ge(sem("y_copied"), 2 * b + 2)
                sp.dma_start(t["out"][0, b * P:(b + 1) * P, :], yt[:, b, :]).then_inc(sem("y_out"), 16)
            sp.wait_ge(sem("y_out"), 16 * TB)

        @block.gpsimd
        def _(pool):
            pool.memset(ones[:, :], 1.0).then_inc(sem("ones_set"), 1)

            pool.wait_ge(sem("setup_copied"), 1 + KD)
            pool.memset(up[:, :, 0:PPAD], 0.0).then_inc(sem("att_zero"), 1)
            pool.memset(kbd[:, :], 0.0).then_inc(sem("att_zero"), 1)
            pool.memset(vbd[:, :, :], 0.0).then_inc(sem("att_zero"), 1)
            for dst, src in ((w2c[:, 0], t["cmp_k_w2"][0]), (w2c[:, 1], t["cmp_v_w2"][0]), (cbias[:, :, :], t["cbias"]),
                             (cvalid[:, :, :], t["cvalid"]), (dist[:, :], t["dist"]), (slopes[:, :], t["slopes"]),
                             (pinv[:, :], t["pinv"])):
                pool.dma_start(dst, src).then_inc(sem("att_consts"), 16)
            pool.wait_ge(sem("att_consts"), 16 * 7)
            pool.wait_ge(sem("att_zero"), 1)

            own = Chain(pool, sem("pool_seq"))

            def stage(u, r, g, first):
                if not first:
                    h = slice(g * DH, (g + 1) * DH)
                    pool.wait_ge(sem("staged"), u)
                    pool.wait_ge(sem("s_ready"), u - 1)
                    own.link(pool.tensor_copy(q_st[0][h, :], q_hi[h, bass.ds(r, 1), :]))
                    pool.wait_ge(sem("nmax_ready"), u - 1)
                own.link(pool.tensor_copy(slope_st[:, g:g + 1], slopes[:, bass.ds(r + g * HPG, 1)]))
                pool.tensor_tensor(biast[:, g, :], dist[:, :], slope_st[:, g:g + 1].broadcast_to([P, S]), ALU.mult)\
                    .then_inc(sem("staged"), 1)

            def stage_rest(b):
                with pool.Fori(0, HPG - 1) as r:
                    own.loop(r, 2 * GR)
                    for g in range(GR):
                        stage(2 * r + (8 * b + g + 2), r + 1, g, False)
                    own.done(HPG - 1)

            for g in range(GR):
                stage(g, 0, g, True)

            for gi in range(4):
                pool.wait_ge(bank_free, T0["u"] + gi + 5)
                src, lo, w = up[:, gi], 0, 2 << gi
                for lev in range(gi + 1):
                    step = 1 << lev
                    lo += step
                    dst = wsum[:, lev % 2]
                    own.link(pool.tensor_tensor(dst[:, lo:], src[:, lo:], src[:, lo - step:PPAD + S - step], ALU.add))
                    src = dst
                pool.tensor_scalar(src[:, PPAD + w:], src[:, PPAD + w:], 1.0 / w, None, ALU.mult)
                own.link(pool.tensor_tensor(src[:, PPAD:PPAD + w], src[:, PPAD:PPAD + w], pinv[:, 0:w], ALU.mult))
                pool.tensor_tensor(up[:, gi, PPAD:], src[:, PPAD:], up[:, gi, PPAD:], ALU.subtract)\
                    .then_inc(sem("d_ready"), 1)
                pool.wait_ge(sem("d_ready"), gi + 1)
            stage_rest(0)
            for g in range(GR):
                pool.wait_ge(sem("nmax_ready"), 7 + g)
                stage(8 + g, 0, g, True)
            stage_rest(1)

            pool.wait_ge(sem("tap_hi"), 1)
            own.link(pool.tensor_tensor(tap_lo[:, :], par[:, P:P + CONV * KD], tap_hi[:, :].bitcast(F32),
                                        ALU.subtract))
            pool.memset(zsum[:, :], 0.0).then_inc(sem("zsum_ready"), 1)

            def add_channels(m):
                pool.wait_ge(sem("zc_ready"), m + 3)
                pool.wait_ge(sem("zsum_ready"), m + 1)
                pool.tensor_tensor(zsum[:, :].unsqueeze(1), zsum[:, :].unsqueeze(1), zc[:, bass.ds(m, 1), :], ALU.add)\
                    .then_inc(sem("zsum_ready"), 1)

            def diagonals(i, j, first=False):
                m = 2 * i + j
                n = N0["pw1"] + j + 1
                pool.wait_ge(hi_done, 2 * i + (n + 1))
                pool.wait_ge(split_done, 2 * i + n)
                pool.tensor_tensor(wlo[:, n % 2], raw[:, n % 2], whi[:, n % 2].bitcast(F32), ALU.subtract)\
                    .then_inc(split_done, 1)
                pool.wait_ge(sem("conv_done"), m + 1)
                for src, dst in ((tap_hi, diag_hi), (tap_lo, diag_lo)):
                    w = src[:, :].bitcast(F32).rearrange("p (t m) -> p t m", m=KD)[:, 0:PETAPS, bass.ds(m, 1)]
                    ins = pool.tensor_tensor(dst[:, j], ident[:, :].unsqueeze(1).broadcast_to([P, PETAPS, P]),
                                             w.broadcast_to([P, PETAPS, P]), ALU.mult)
                ins.then_inc(sem("diag_ready"), 1)
                pool.wait_ge(sem("z_hi"), m + 1)
                pool.tensor_tensor(z_lo[:, j], z[:, j], z_hi[:, j].bitcast(F32), ALU.subtract)\
                    .then_inc(sem("z_lo"), 1)
                if not first:
                    add_channels(m - 1)

            diagonals(0, 0, True)
            diagonals(0, 1)
            with pool.Fori(1, 4) as i:
                for j in range(2):
                    diagonals(i, j)
            add_channels(KD - 1)

            pool.wait_ge(bank_free, T0["qk2"] + 4)
            pool.dma_start(wgu[:, :], t["w_gate_up_2"][0]).then_inc(sem("gla_consts"), 16)
            pool.dma_start(glm[:, :, :], t["glm"]).then_inc(sem("gla_consts"), 16)
            pool.memset(scan1[:, :], 1.0).then_inc(sem("gla_set"), 1)
            pool.memset(ccx[:, :, 0:2], 0.0).then_inc(sem("gla_set"), 1)
            pool.wait_ge(sem("gla_set"), 2)
            pool.memset(scan1[:, :].rearrange("p (c t) -> p c t", t=CH)[:, :, 0:1], 0.0).then_inc(sem("gla_set"), 1)

            pool.memset(at[:, :, :], 0.0).then_inc(sem("at_zero"), 1)

            def distance(lev):
                m = LEVELS[lev] if lev < len(LEVELS) else CH // 2
                last = m - 1 if lev < len(LEVELS) else CH - 1
                pool.wait_ge(sem("bc_ready"), 1)
                if lev:
                    pool.wait_ge(sem("ex_ready"), lev)
                b3, d3 = (v[:, :].rearrange("p (b t) -> p b t", t=2 * m) for v in (bc, dd))
                ends = b3[:, :, last:last + 1].broadcast_to([P, 2 * S // (2 * m), 2 * m])
                pool.tensor_tensor(d3, *((b3, ends) if lev < len(LEVELS) else (ends, b3)), ALU.subtract)\
                    .then_inc(sem("dd_ready"), 1)
                pool.wait_ge(sem("dd_ready"), lev + 1)

            def short_conv(k):
                pool.wait_ge(sem("ccx_ready"), k + 1)
                for tap in range(3):
                    col = COL["conv_w_2"] + tap * 4 + k
                    own.link(pool.tensor_tensor(t3[:, min(tap, 1)], ccx[:, k % 2, tap:tap + S],
                                                par[:, col:col + 1].broadcast_to([P, S]), ALU.mult))
                    if tap:
                        own.link(pool.tensor_tensor(t3[:, 0], t3[:, 0], t3[:, 1], ALU.add))
                pool.tensor_tensor(cbt[:, k], cbt[:, k], t3[:, 0], ALU.mult).then_inc(sem("yc_ready"), 1)
                pool.wait_ge(sem("yc_ready"), k + 1)

            for lev in range(5):
                distance(lev)
            short_conv(0)
            distance(5)
            short_conv(1)
            distance(6)
            short_conv(2)
            short_conv(3)

            pool.wait_ge(panel_done, N0["ple"])
            pool.dma_start(ptok[:, :, :], t["p_2"][0, 0].rearrange("(b p) c -> p b c", p=P))\
                .then_inc(sem("p_in"), 16)

        @block.scalar
        def _(act):
            seq = Chain(act, sem("act_seq"))

            def hi(n, i=0):
                act.wait_ge(raw_full[n % 2], 32 * i + 32 * (n // 2 + 2))
                if n >= 2:
                    act.wait_ge(panel_done, 2 * i + (n - 1))
                act.activation(whi[:, n % 2], raw[:, n % 2], ACT.Copy).then_inc(hi_done, 1)

            def square(q, k, src, kk=None):
                if q or k >= 2:
                    act.wait_ge(sem("sq_added"), k + (8 * q - 1))
                act.activation(sq[:, (k if kk is None else kk) % 2], src, ACT.Square).then_inc(sem("sq_ready"), 1)

            def cast(dst, src, name, scale=1.0):
                act.activation(dst, src, ACT.Copy, scale=scale).then_inc(sem(name), 1)

            def gain(q, k):
                return par[:, bass.ds(NORMS[q] + k, 1)]

            def root(q):
                act.wait_ge(sem("sumsq"), q + 1)
                act.activation(rstd[:, :], ps[4][:, :], ACT.Sqrt, bias=(eps5 if q == LN else eps6)[:, :],
                               scale=1.0 / D).then_inc(sem("std_ready"), 1)

            def root_tokens(q):
                act.wait_ge(sem("sumsq"), q + 1)
                act.activation(tok_rstd, ps[4][:, 0:TB], ACT.Sqrt, bias=(eps5 if q == LN else eps6)[:, :],
                               scale=1.0 / D).then_inc(sem("std_ready"), 1)

            act.wait_ge(sem("prow_zero"), 1)
            for name, rows in PARAMS:
                src = t[name].rearrange("a b -> (a b)") if len(t[name].shape) == 2 else t[name]
                act.dma_start(prow[COL[name]:COL[name] + rows, 0, :],
                              src.rearrange("(r c) -> r c", c=P)).then_inc(sem("params_in"), 16)
            hi(0)
            act.wait_ge(sem("consts_set"), 1)
            for k in range(2):
                act.wait_ge(sem("setup_copied"), k + 1)
                square(MIX, k, x[:, k])
            act.wait_ge(sem("setup_copied"), KD + 1)
            for k in range(KD):
                cast(act_hi[:, k], x[:, k], f"xhi{MIX}", gain(MIX, k))
                if k >= 2:
                    square(MIX, k, x[:, k])
            root(MIX)

            for i in range(2):
                hi(N0["q"] + i + 1)
                for k in (2 * i, 2 * i + 1):
                    act.wait_ge(bank_free, T0["q"] + k + 5)
                    cast(q_hi[:, k], q_f[:, k], "q_hi")
            hi(N0["kvc"] + 1)
            hi(N0["gate"] + 1)
            act.wait_ge(bank_free, T0["gate"] + 5)
            act.activation(gsig, t1[0:24, 0], ACT.Sigmoid).then_inc(sem("gate_sig"), 1)
            for i in range(2):
                hi(N0["u"] + i + 1)
            for j, name in enumerate(("ck", "cv")):
                act.wait_ge(sem("cmp_set"), j + 1)
                if j:
                    act.wait_ge(panel_done, N0["cv"])
                cast(cmp_hi[:, :, :], cmpf[:, :, :], "cmp_hi")
                hi(N0[name] + 1)
                act.wait_ge(bank_free, T0[name] + 5)
                act.activation(ghid[:, j], t1[:, j, 0:62], ACT.Gelu_apprx_tanh).then_inc(sem("ghid_ready"), 1)
            def keys(br, name):
                act.wait_ge(bank_free, T0[name] + 5)
                cast(k_hi[:, br], k_f[:, br], "k_hi")

            act.wait_ge(sem("kbd_ready"), 1)
            cast(kbd_hi[:, :], kbd[:, :], "kbd_hi")
            hi(N0["kvs"] + 1)
            keys(0, "kvs")
            act.wait_ge(sem("c_shifted"), 1)
            act.activation(s_sb[:, 0, 0:1024], s_sb[:, 0, 0:1024], ACT.Exp).then_inc(sem("c_exp"), 1)
            hi(N0["kvw"] + 1)
            keys(1, "kvw")
            act.wait_ge(sem("c_pv"), 2)
            act.activation(acc[:, 1], ps[1][:, :], ACT.Copy)
            act.wait_ge(sem("c_pv"), 4)
            act.activation(acc[:, 3], ps[3][:, :], ACT.Copy).then_inc(sem("pt_a"), 1)

            def exps(u, g):
                act.wait_ge(sem("nmax_ready"), u + 1)
                for qb in range(TB):
                    w = (qb + 1) * P
                    e = s_sb[:, g, OFF[qb]:OFF[qb] + w]
                    ins = act.activation(e, e, ACT.Exp, bias=nmx[:, g, qb:qb + 1], accum_out=sm[:, g, qb:qb + 1])
                ins.then_inc(sem("p_ready"), 1)

            def stage_lo(u, r, g):
                act.wait_ge(sem("s_ready"), u - 1)
                h = slice(g * DH, (g + 1) * DH)
                cast(q_st[1][h, :].unsqueeze(1), q_lo[h, bass.ds(r, 1), :], "lo_staged")

            def copy_pt(u, g):
                act.wait_ge(sem("pt_ready"), 3 * u + 1)
                act.wait_ge(sem("pv_ready"), u + 1)
                act.activation(pt[:, 0:512], ps[6][:, :], ACT.Copy).then_inc(sem("pt_a"), 1)
                act.wait_ge(sem("pt_ready"), 3 * u + 2)
                act.activation(pt[:, 1024:1280], ps[3 * g + 2][:, 256:512], ACT.Copy).then_inc(sem("pt_a"), 1)

            for gi in range(4):
                act.wait_ge(sem("d_ready"), gi + 1)
                cast(act_hi[:, 4 + gi], up[:, gi, PPAD:], "d_hi")
            exps(0, 0)
            for gi in range(4):
                act.wait_ge(bank_free, T0["pool"] + gi + 5)
                cast(act_hi[:, 4 + gi], y_f[gi], "y_hi")
            for b in range(2):
                with act.Fori(0, HPG - 1) as r:
                    for g in range(GR):
                        stage_lo(2 * r + (8 * b + g + 2), r + 1, g)
                        copy_pt(2 * r + (8 * b + g), g)
                        exps(2 * r + (8 * b + g + 1), 1 - g)
                copy_pt(8 * b + 6, 0)
                exps(8 * b + 7, 1)
                copy_pt(8 * b + 7, 1)
                if b == 0:
                    exps(8, 0)
            hi(N0["pool"] + 1)
            for k in range(4):
                act.wait_ge(sem("oT_ready"), k + 1)
                cast(act_hi[:, k], ps[4 + k][:, :], "o_hi")

            def late(q, name, extra=None):
                for i in range(4):
                    hi(N0[name] + i + 1)
                    for k in (2 * i, 2 * i + 1):
                        act.wait_ge(bank_free, T0[name] + k + 5)
                        square(q, k, x[:, k])
                act.wait_ge(panel_done, N0[name] + 4)
                for k in range(KD):
                    cast(act_hi[:, k], x[:, k], f"xhi{q}", gain(q, k))

            late(FFN1, "mix")

            def ffn(f, q, up_, dn, qn):
                root(q)
                with act.Fori(0, KF // 2) as i:
                    for j in range(2):
                        hi(N0[up_] + j + 1, i)
                        act.wait_ge(bank_free, 4 * i + (T0[up_] + 2 * j + 5))
                        act.activation(t3[:, j], t1[:, j], ACT.Silu).then_inc(sem("silu_ready"), 1)
                        act.wait_ge(sem("hidden_set"), 2 * i + (KF * f + j + 1))
                        cast(hid_hi[:, bass.ds(2 * i + j, 1), :], t1[:, j], "hidden_hi")
                with act.Fori(0, 2) as i:
                    for j in range(4):
                        for h in range(2):
                            hi(N0[dn] + 2 * j + h + 1, 4 * i)
                        act.wait_ge(bank_free, 4 * i + (T0[dn] + j + 5))
                        square(qn, 4 * i + j, x[:, bass.ds(4 * i + j, 1), :], j)
                        if qn != FINAL:
                            cast(act_hi[:, bass.ds(4 * i + j, 1), :], x[:, bass.ds(4 * i + j, 1), :],
                                 f"xhi{qn}", gain(qn, 4 * i + j))

            ffn(0, FFN1, "up1", "dn1", CONVIN)

            root(CONVIN)
            act.wait_ge(panel_done, N0["pw1"])
            cast(tap_hi[:, :], par[:, P:P + CONV * KD], "tap_hi")
            with act.Fori(0, 4) as i:
                for j in range(2):
                    hi(N0["pw1"] + j + 1, i)
                    act.wait_ge(bank_free, 4 * i + (T0["pw1"] + 2 * j + 6))
                    act.activation(t3[:, j], t2[:, j], ACT.Sigmoid,
                                   bias=par[:, bass.ds(2 * i + (COL["conv_b_pw1"] + 8 + j), 1)])\
                        .then_inc(sem("glu_sig"), 1)
                    act.wait_ge(sem("z_ready"), 2 * i + (j + 1))
                    act.wait_ge(sem("conv_done"), 2 * i + (j + 1))
                    cast(z_hi[:, j], z[:, j], "z_hi")
            for k in range(KD):
                act.wait_ge(sem("ln_centered"), k + 1)
                square(LN, k, zc[:, k])
            root_tokens(LN)
            for k in range(KD):
                act.wait_ge(sem("ln_scaled"), k + 1)
                seq.link(act.activation(t3[:, k % 2], t1[:, k % 2], ACT.Silu,
                                        scale=par[:, COL["conv_ln_g"] + k:COL["conv_ln_g"] + k + 1],
                                        bias=par[:, COL["conv_ln_b"] + k:COL["conv_ln_b"] + k + 1]))
                cast(act_hi[:, k], t3[:, k % 2], "zhi")
            late(FFN2, "pw2")
            ffn(1, FFN2, "up2", "dn2", FINAL)
            root_tokens(FINAL)
            hi(N0["glr"] + 1)
            for k in range(KD):
                act.wait_ge(sem("x_final"), k + 1)
                square(GLAIN, k, x[:, k])
                cast(act_hi[:, k], x[:, k], f"xhi{GLAIN}", gain(GLAIN, k))
            root_tokens(GLAIN)

            def decay(lev):
                act.wait_ge(sem("dd_ready"), lev + 1)
                if lev:
                    act.wait_ge(sem("kd_ready"), lev)
                seq.link(act.activation(ex[:, :], dd[:, :], ACT.Abs))
                act.activation(ex[:, :], ex[:, :], ACT.Exp, scale=-1.0).then_inc(sem("ex_ready"), 1)

            for i in range(2):
                hi(N0["qk2"] + i + 1)
            act.wait_ge(sem("logit_ready"), 2)
            seq.link(act.activation(la2[:, :], la[:, :], ACT.Abs))
            seq.link(act.activation(la2[:, :], la2[:, :], ACT.Exp, scale=-1.0))
            act.activation(la2[:, :], la2[:, :], ACT.Ln, bias=1.0).then_inc(sem("softplus_ready"), 1)
            for i in range(2):
                hi(N0["v2"] + i + 1)
            decay(0)
            for i in range(2):
                hi(N0["cb2"] + i + 1)
                decay(1 + i)
            for i in range(3):
                hi(N0["ccx"] + i + 1)
                decay(3 + i)
            hi(N0["ccx"] + 4)
            act.wait_ge(sem("dd_ready"), len(LEVELS) + 1)
            act.wait_ge(sem("kd_ready"), len(LEVELS))
            act.activation(ex[:, :], dd[:, :], ACT.Exp).then_inc(sem("ex_ready"), 1)
            act.activation(la2[:, :], bc[:, :], ACT.Exp).then_inc(sem("ebc_ready"), 1)

            def gate_tile(k):
                act.wait_ge(bank_free, T0["g2"] + k + 5)
                act.activation(gs[:, k], gs[:, k], ACT.Silu).then_inc(sem("gs_ready"), 1)

            hi(N0["g2"] + 1)
            gate_tile(0)
            gate_tile(1)
            hi(N0["g2"] + 2)
            for h in range(GH):
                act.wait_ge(sem("go_copied"), h + 1)
                act.activation(osq[h], gla_o[:, h], ACT.Square).then_inc(sem("osq_ready"), 1)
            gate_tile(2)
            act.wait_ge(sem("go_sum"), 1)
            act.activation(head_rstd[:, :], ps[4][:, 0:GH * TB], ACT.Sqrt, bias=eps6[:, :], scale=1.0 / GDV)\
                .then_inc(sem("go_std"), 1)
            gate_tile(3)
            for k in range(4):
                act.wait_ge(sem("yc_ready"), k + 1)
                cast(act_hi[:, 4 + k], cbt[:, k], "yc_hi")
            for h in range(GH):
                act.wait_ge(sem("go_out"), h + 1)
                cast(act_hi[:, h], t1[:, h % 2], "go_hi")
            late(FFN3, "mix2")
            ffn(2, FFN3, "up3", "dn3", PLE)

            root(PLE)
            for c in range(2):
                act.wait_ge(sem("pf_ready"), c + 1)
                cast(pf_hi[:, c], ps[5 + c][:, :], "pf_hi")

            def ple(i, j, more):
                if more:
                    hi(N0["ple"] + j + 1, i)
                act.wait_ge(bank_free, 4 * i + (T0["ple"] + 2 * j + 5))
                act.activation(t3[:, j], t1[:, j], ACT.Sigmoid).then_inc(sem("ple_sig"), 1)
                act.wait_ge(sem("ple_x"), 2 * i + (j + 1))
                square(OUT, 2 * i + j, x[:, bass.ds(2 * i + j, 1), :], j)

            with act.Fori(0, 3) as i:
                for j in range(2):
                    ple(i, j, True)
            ple(3, 0, True)
            ple(3, 1, False)
            root_tokens(OUT)

        @block.tensor
        def _(pe):
            def mm3(out, lhs, rhs, start, stop):
                pe.matmul(out, lhs[0], rhs[0], start=start, stop=False)
                pe.matmul(out, lhs[0], rhs[1], start=False, stop=False)
                return pe.matmul(out, lhs[1], rhs[0], start=False, stop=stop)

            def slot(n, k, width=256, c0=0):
                a = slice(k * width + c0, k * width + c0 + P)
                return whi[:, n % 2, a], wlo[:, n % 2, a]

            def act_k(k):
                return act_hi[:, k], act_lo[:, k]

            def tile(T, i4, lhs, rhs, ks, sig, start=True, stop=True, act_wait=None):
                if start:
                    pe.wait_ge(bank_free, i4 + (T + 1))
                for k in ks:
                    if act_wait:
                        pe.wait_ge(*(act_wait(k) if callable(act_wait) else (sem(act_wait), k + 1)))
                    ins = mm3(bank(T)[:, :], lhs(k), rhs(k), start and k == ks[0], stop and k == ks[-1])
                ins.then_inc(sig, 1)

            def panel2(name, j, i=0, lhs=None, act_wait=None, after=None, ks=range(KD)):
                n, T = N0[name] + j, T0[name] + 2 * j
                pe.wait_ge(split_done, 2 * i + (n + 1))
                for c in range(2):
                    f = lhs(n, c) if lhs else (lambda k: slot(n, k, 256, c * P))
                    tile(T + c, 4 * i, f, act_k, ks, panel_done if c else tile_done,
                         act_wait=act_wait if c == 0 else None)
                    if c == 0 and after:
                        after()

            def sumsq(q):
                pe.wait_ge(sem("sq_added"), 8 * q + 8)
                pe.matmul(ps[4][:, :], ones[:, :], sqacc[:, :], start=True, stop=True).then_inc(sem("sumsq"), 1)

            def sums_of_tokens(q):
                pe.wait_ge(sem("sq_added"), 8 * q + 8)
                for b in range(TB):
                    ins = pe.matmul(ps[4][:, b:b + 1], sqacc[:, b * P:(b + 1) * P], ones[:, 0:1], start=True, stop=True)
                ins.then_inc(sem("sumsq"), 1)

            def repeat_rstd(count):
                pe.wait_ge(sem("tok_inv"), count)
                for b in range(TB):
                    ins = pe.matmul(ps[5][:, b * P:(b + 1) * P], tok_rstd[:, b:b + 1].broadcast_to([P, P]),
                                    ident[:, :], start=True, stop=True)
                ins.then_inc(sem("rstd_repeated"), 1)

            pe.wait_ge(sem("ident_in"), 16)
            pe.wait_ge(sem("x_in"), 16 * TB)
            for k in range(KD):
                if k >= 4:
                    pe.wait_ge(sem("setup_copied"), k - 3)
                for b in range(TB):
                    ins = pe.transpose(ps[4 + k % 4][:, b * P:(b + 1) * P], xt[:, b, k * P:(k + 1) * P], ident[:, :])
                ins.then_inc(sem("setup_ready"), 1)
            pe.wait_ge(sem("params_in"), 16 * len(PARAMS))
            pe.wait_ge(sem("taps_in"), 16 * 5)
            pe.wait_ge(sem("setup_copied"), 5)
            for b in range(4):
                ins = pe.transpose(ps[4][:, b * P:(b + 1) * P], prow[:, b], ident[:, :])
            ins.then_inc(sem("setup_ready"), 1)

            pe.wait_ge(sem("ones_set"), 1)
            for i in range(2):
                panel2("q", i, act_wait=f"act{MIX}" if i == 0 else None,
                       after=(lambda: sumsq(MIX)) if i == 0 else None)
            panel2("kvc", 0)
            n = N0["gate"]
            pe.wait_ge(split_done, n + 1)
            tile(T0["gate"], 0, lambda k: slot(n, k), act_k, range(KD), panel_done)
            panel2("u", 0)
            pe.wait_ge(sem("gate_sig"), 1)
            for b in range(TB):
                ins = pe.transpose(ps[7][:, b * 24:(b + 1) * 24], gsig[:, b * P:(b + 1) * P], ident[0:24, 0:24])
            ins.then_inc(sem("gT_ready"), 1)
            panel2("u", 1)

            for j, name in enumerate(("ck", "cv")):
                n, T = N0[name], T0[name]
                pe.wait_ge(split_done, n + 1)
                pe.wait_ge(sem("cmp_lo"), j + 1)
                pe.wait_ge(bank_free, T + 1)
                for k in range(16):
                    ins = mm3(bank(T)[:, 0:62], slot(n, k, P), (cmp_hi[:, k], cmp_lo[:, k]), k == 0, k == 15)
                ins.then_inc(panel_done, 1)
                pe.wait_ge(sem("ghid_ready"), j + 1)
                pe.wait_ge(sem("att_consts"), 16 * 7)
                if j == 0:
                    pe.matmul(ps[4][0:DH, 0:62], w2c[:, 0], ghid[:, 0], start=True, stop=True)\
                        .then_inc(sem("kcmp_ready"), 1)
                else:
                    for g in range(GR):
                        ins = pe.matmul(ps[5][0:NCMP, g * DH:(g + 1) * DH], ghid[:, 1, g * NCMP:(g + 1) * NCMP],
                                        w2c[:, 1], start=True, stop=True)
                    ins.then_inc(sem("vcmp_ready"), 1)
            panel2("kvs", 0)
            pe.wait_ge(sem("kbd_lo"), 1)
            pe.wait_ge(sem("vbd_ready"), 1)
            for b in range(TB):
                for r in range(HPG):
                    out = ps[4 + b // 2][:, (b % 2) * 256:(b % 2 + 1) * 256].rearrange("p (g r n) -> p g r n", g=GR, r=HPG)
                    qs = slice(b * P, (b + 1) * P)
                    ins = mm3(out[:, :, r, :], (q_hi[:, r, qs], q_lo[:, r, qs]), (kbd_hi[:, :], kbd_lo[:, :]),
                              True, True)
            ins.then_inc(sem("c_scores"), 1)

            def values(br, name):
                pe.wait_ge(bank_free, T0[name] + 6)
                for kb in range(TB):
                    ins = pe.transpose(ps[6 + br][:, kb * P:(kb + 1) * P], vf[:, br, kb * P:(kb + 1) * P], ident[:, :])
                ins.then_inc(sem("vT_ready"), 1)

            panel2("kvw", 0, after=lambda: values(0, "kvs"))
            pe.wait_ge(sem("c_probs"), 1)
            for g in range(GR):
                for b in range(TB):
                    ins = pe.transpose(ps[4 + g][:, b * P:(b + 1) * P],
                                       s_sb[:, 0, b * 256 + g * P:b * 256 + (g + 1) * P], ident[:, :])
            ins.then_inc(sem("c_pT"), 1)
            values(1, "kvw")
            pe.wait_ge(sem("c_pT_copied"), 1)
            pe.wait_ge(bank_free, T0["pool"] + 4)
            for b in range(TB):
                for g in range(GR):
                    ins = pe.matmul(ps[b][:, g * 256:(g + 1) * 256], pc_t[:, g, b * P:(b + 1) * P], vbd[:, g],
                                    start=True, stop=True)
                ins.then_inc(sem("c_pv"), 1)

            def scores(u, b, g, first=False):
                pe.wait_ge(sem("staged"), u + 1)
                if not first:
                    pe.wait_ge(sem("lo_staged"), u - (2 * b + 1))
                h = slice(g * DH, (g + 1) * DH)
                for qb, bk, c in ((3, 0, 0), (2, 1, 0), (0, 1, 384), (1, 2, 0)):
                    if qb == 1 and (b or not first):
                        pe.wait_ge(sem("pt_a"), 2 * u - 1)
                    qs = slice(qb * P, (qb + 1) * P)
                    lhs = (q_hi[h, 0, qs], q_lo[h, 0, qs]) if first else (q_st[0][h, qs], q_st[1][h, qs])
                    ins = mm3(ps[3 * g + bk][:, c:c + (qb + 1) * P], lhs,
                              (k_hi[h, b, 0:(qb + 1) * P], k_lo[h, b, 0:(qb + 1) * P]), True, True)
                ins.then_inc(sem("s_ready"), 1)

            def output(u, b, g, then=None):
                def pT(kb, bk, c):
                    for qb in range(kb, TB):
                        o = OFF[qb] + kb * P
                        ins = pe.transpose(ps[bk][:, c + (qb - kb) * P:c + (qb - kb + 1) * P],
                                           s_sb[:, g, o:o + P], ident[:, :])
                    return ins
                pe.wait_ge(sem("p_ready"), u + 1)
                pe.wait_ge(sem("pt_a"), 2 * u + 1)
                pT(0, 6, 0).then_inc(sem("pt_ready"), 1)
                pT(2, 3 * g + 2, 256).then_inc(sem("pt_ready"), 1)
                pe.wait_ge(sem("pv_out"), u + 1)
                pT(1, 7, 0)
                pT(3, 7, 384).then_inc(sem("pt_ready"), 1)
                if then:
                    then()
                pe.wait_ge(sem("pt_v"), u + 1)
                pe.wait_ge(sem("pt_a"), 2 * u + 3)
                start_of = {0: 0, 1: 512, 3: 896, 2: 1024}
                for qb in range(TB):
                    for kb in range(qb + 1):
                        o = start_of[kb] + (qb - kb) * P
                        ins = pe.matmul(ps[7][:, qb * DH:(qb + 1) * DH], pt[:, o:o + P],
                                        v_tm[:, b, kb, g * DH:(g + 1) * DH], start=kb == 0, stop=kb == qb)
                ins.then_inc(sem("pv_ready"), 1)

            pe.wait_ge(sem("c_done"), 1)
            pe.wait_ge(sem("pt_a"), 1)
            for g in range(GR):
                scores(g, 0, g, True)
            n = N0["pool"]
            pe.wait_ge(split_done, n + 1)
            for gi in range(4):
                pe.wait_ge(sem("d_lo"), gi + 1)
                if gi >= 2:
                    pe.wait_ge(bank_free, T0["pool"] + gi + 3)
                mm3(ps[6 + gi % 2][:, :], slot(n, gi, P), act_k(4 + gi), True, True)\
                    .then_inc(sem("pooled") if gi < 3 else panel_done, 1)
            pe.wait_ge(bank_free, T0["pool"] + 8)
            for b in range(2):
                with pe.Fori(0, HPG - 1) as r:
                    for g in range(GR):
                        output(2 * r + (8 * b + g), b, g, lambda: scores(2 * r + (8 * b + g + 2), b, g))
                for g in range(GR):
                    output(8 * b + 6 + g, b, g, (lambda: scores(8 + g, 1, g, True)) if b == 0 else None)

            pe.wait_ge(sem("pv_out"), 17)
            for k in range(4):
                for b in range(TB):
                    ins = pe.transpose(ps[4 + k][:, b * P:(b + 1) * P], acc[:, b, k * P:(k + 1) * P], ident[:, :])
                ins.then_inc(sem("oT_ready"), 1)

            panel2("mix", 0, ks=[4, 5, 6, 7, 0, 1, 2, 3],
                   act_wait=lambda k: (sem("y_lo"), k - 3) if k >= 4 else (sem("o_lo"), k + 1))
            panel2("mix", 1)
            with pe.Fori(1, 2) as i:
                for j in range(2):
                    panel2("mix", j, i)

            def ffn(f, q, up_, dn):
                panel2(up_, 0, act_wait=f"act{q}", after=lambda: sumsq(q))
                panel2(up_, 1)
                with pe.Fori(1, KF // 2) as i:
                    for j in range(2):
                        panel2(up_, j, i)
                n, T = N0[dn], T0[dn]
                with pe.Fori(0, 2) as i:
                    for j in range(4):
                        for h in range(2):
                            m = n + 2 * j + h
                            pe.wait_ge(split_done, 8 * i + (m + 1))
                            pe.wait_ge(sem("hidden_lo"), KF * f + KHALF * (h + 1))
                            tile(T + j, 4 * i, lambda k: slot(m, k, P),
                                 lambda k: (hid_hi[:, h * KHALF + k], hid_lo[:, h * KHALF + k]),
                                 range(KHALF), panel_done, start=h == 0, stop=h == 1)

            ffn(0, FFN1, "up1", "dn1")

            panel2("pw1", 0, act_wait=f"act{CONVIN}", after=lambda: sumsq(CONVIN))
            panel2("pw1", 1)

            def convolve(m, j):
                pe.wait_ge(sem("diag_ready"), m + 1)
                pe.wait_ge(sem("z_lo"), m + 1)
                pe.wait_ge(sem("zc_ready"), m + 1)
                for tap in range(PETAPS):
                    ins = mm3(ps[5 + j][:, :], (diag_hi[:, j, tap, :], diag_lo[:, j, tap, :]),
                              (z_hi[:, j, tap:tap + S], z_lo[:, j, tap:tap + S]), tap == 0, tap == PETAPS - 1)
                ins.then_inc(sem("conv_done"), 1)

            convolve(0, 0)
            with pe.Fori(1, 4) as i:
                for j in range(2):
                    panel2("pw1", j, i)
                    convolve(2 * i + (j - 1), 1 - j)
            convolve(KD - 1, 1)
            pe.wait_ge(sem("zsum_ready"), KD + 1)
            pe.matmul(ps[7][:, :], ones[:, :], zsum[:, :], start=True, stop=True).then_inc(sem("zmean_ready"), 1)
            sums_of_tokens(LN)
            repeat_rstd(1)
            panel2("pw2", 0, act_wait="zlo")
            panel2("pw2", 1)
            with pe.Fori(1, 2) as i:
                for j in range(2):
                    panel2("pw2", j, i)
            ffn(1, FFN2, "up2", "dn2")

            sums_of_tokens(FINAL)
            repeat_rstd(2)
            n = N0["glr"]
            pe.wait_ge(split_done, n + 1)
            tile(T0["glr"], 0, lambda k: slot(n, k), act_k, range(KD), panel_done, act_wait=f"act{GLAIN}")
            sums_of_tokens(GLAIN)
            panel2("qk2", 0, after=lambda: repeat_rstd(3))
            pe.wait_ge(bank_free, T0["glr"] + 5)
            pe.wait_ge(sem("gla_consts"), 32)
            for c in range(2):
                pe.matmul(ps[4 + c][:, :], wgu[:, c * P:(c + 1) * P], glr[:, :], start=True, stop=True)\
                    .then_inc(sem("logit_mm"), 1)
            panel2("qk2", 1)

            def values(half):
                if half:
                    pe.wait_ge(sem("v2_copied"), 2)
                else:
                    pe.wait_ge(bank_free, T0["v2"] + 8)
                    pe.wait_ge(sem("logit_ready"), 2)
                for w in (2 * half, 2 * half + 1):
                    for h in range(GH):
                        ins = pe.transpose(ps[4 + w % 2][:, h * P:(h + 1) * P], v2f[:, h, w * P:(w + 1) * P],
                                           ident[:, :])
                    ins.then_inc(sem("v2T_ready"), 1)

            def head(h):
                return slice((h % 2) * GDK, (h % 2 + 1) * GDK), h // 2, (h % 2) * 2 + h // 2

            def self_scores(half):
                pe.wait_ge(sem("v2_copied"), TB)
                if half:
                    pe.wait_ge(sem("self_added"), 2)
                for h in (half, half + 2):
                    part, c, a = head(h)
                    for w in range(TB):
                        ins = pe.matmul(ps[4 + c][:, w * P:(w + 1) * P], k2[part, c, w * P:(w + 1) * P],
                                        q2[part, c, w * P:(w + 1) * P], start=True, stop=True)
                    ins.then_inc(sem("self_scores"), 1)

            def level(lev):
                m = LEVELS[lev]
                pe.wait_ge(sem("kd_ready"), lev + 1)
                if lev:
                    pe.wait_ge(sem("lev_added"), 2 * lev)
                for h in (0, 2, 1, 3):
                    part, c, a = head(h)
                    for w in range(TB):
                        o = c * S + w * P
                        right = qd[part, o:o + P].rearrange("p (b t) -> p b t", t=2 * m)[:, :, m:]
                        out = ps[6 + h % 2][:, (c * TB + w) * CH:(c * TB + w + 1) * CH]
                        ins = pe.matmul(out, kd[part, o:o + P], right, start=True, stop=True)
                    if c == 1:
                        ins.then_inc(sem("lev_scores"), 1)

            def updates(chunks):
                pe.wait_ge(sem("kdt_copied"), 2)
                pe.wait_ge(sem("lev_added"), 2 * len(LEVELS))
                for ch in chunks:
                    w, part = ch // 2, slice((ch % 2) * CH, (ch % 2 + 1) * CH)
                    if ch >= 4:
                        pe.wait_ge(sem("state_set"), ch - 3)
                    for c in range(2):
                        ins = pe.matmul(ps[4 + ch % 4][:, c * 256:(c + 1) * 256], kdt[part, w, c, :],
                                        v2[part, w, c * 256:(c + 1) * 256], start=True, stop=True)
                    ins.then_inc(sem("update_ready"), 1)

            def outputs():
                pe.wait_ge(sem("state_set"), NCH - 1)
                for h in range(GH):
                    part, c, a = head(h)
                    for w in range(TB):
                        pe.matmul(ps[4 + h][:, w * P:(w + 1) * P], v2[:, w, h * GDV:(h + 1) * GDV],
                                  at[:, a, w * P:(w + 1) * P], start=w == 0, stop=False, skip_group_check=True)
                    for ch in range(1, NCH):
                        o = c * S + ch * CH
                        ins = pe.matmul(ps[4 + h][:, ch * CH:(ch + 1) * CH], state[part, c, ch, :], qe[part, o:o + CH],
                                        start=False, stop=ch == NCH - 1, skip_group_check=True)
                    ins.then_inc(sem("go_ready"), 1)

            panel2("v2", 0)
            panel2("v2", 1)
            level(0)
            for j in range(2):
                panel2("cb2", j)
                values(j)
                level(1 + j)
            for j in range(2):
                panel2("ccx", j)
                self_scores(j)
                level(3 + j)
            panel2("ccx", 2)
            level(5)
            panel2("ccx", 3)
            pe.wait_ge(sem("kd_ready"), len(LEVELS) + 1)
            for c in range(2):
                for w in range(TB):
                    ins = pe.transpose(ps[4 + c][:, w * P:(w + 1) * P], kd[:, c * S + w * P:c * S + (w + 1) * P],
                                       ident[:, :])
                ins.then_inc(sem("kdT_ready"), 1)
            panel2("g2", 0, after=lambda: updates(range(4)))
            updates(range(4, NCH - 1))
            panel2("g2", 1, after=outputs)
            for h in range(GH):
                pe.wait_ge(sem("osq_ready"), h + 1)
                for b in range(TB):
                    ins = pe.matmul(ps[4][:, h * TB + b:h * TB + b + 1], osq[h][:, b * P:(b + 1) * P], ones[:, 0:1],
                                    start=True, stop=True)
            ins.then_inc(sem("go_sum"), 1)
            pe.wait_ge(sem("go_rstd"), 1)
            for h in range(GH):
                for b in range(TB):
                    c = h * TB + b
                    ins = pe.matmul(ps[4 + (h + 1) % 4][:, b * P:(b + 1) * P],
                                    head_rstd[:, c:c + 1].broadcast_to([P, P]), ident[:, :], start=True, stop=True)
                ins.then_inc(sem("go_scale"), 1)
            panel2("mix2", 0, ks=[4, 5, 6, 7, 0, 1, 2, 3],
                   act_wait=lambda k: (sem("yc_lo"), k - 3) if k >= 4 else (sem("go_lo"), k + 1))
            panel2("mix2", 1)
            with pe.Fori(1, 2) as i:
                for j in range(2):
                    panel2("mix2", j, i)
            ffn(2, FFN3, "up3", "dn3")

            def ple(i, j, **kw):
                n, T = N0["ple"] + j, T0["ple"] + 2 * j
                pe.wait_ge(split_done, 2 * i + (n + 1))
                tile(T, 4 * i, lambda k: slot(n, k, P), act_k, range(KD), tile_done, act_wait=kw.get("act_wait"))
                if kw.get("act_wait"):
                    sumsq(PLE)
                    pe.wait_ge(sem("p_in"), 16)
                    for c in range(2):
                        for b in range(TB):
                            ins = pe.transpose(ps[5 + c][:, b * P:(b + 1) * P], ptok[:, b, c * P:(c + 1) * P],
                                               ident[:, :])
                        ins.then_inc(sem("pf_ready"), 1)
                    pe.wait_ge(sem("pf_done"), 2)
                tile(T + 1, 4 * i, lambda k: slot(n, KD + k, P), lambda k: (pf_hi[:, k], pf_lo[:, k]), range(2),
                     panel_done)

            ple(0, 0, act_wait=f"act{PLE}")
            ple(0, 1)
            with pe.Fori(1, 4) as i:
                for j in range(2):
                    ple(i, j)
            sums_of_tokens(OUT)
            repeat_rstd(4)
            pe.wait_ge(sem("y_ready"), KD)
            pe.wait_ge(bank_free, NTILE + 4)
            for b in range(TB):
                for c in range(2):
                    if b >= 2:
                        pe.wait_ge(sem("y_copied"), 2 * b + c - 3)
                    for k in range(4):
                        ins = pe.transpose(ps[(2 * b + c) % 4][:, k * P:(k + 1) * P],
                                           x[:, 4 * c + k, b * P:(b + 1) * P], ident[:, :])
                    ins.then_inc(sem("yT_ready"), 1)

        @block.vector
        def _(ve):
            seq = Chain(ve, sem("dve_seq"))

            def lo(n, i=0):
                ve.wait_ge(hi_done, 2 * i + (n + 1))
                ve.tensor_tensor(wlo[:, n % 2], raw[:, n % 2], whi[:, n % 2].bitcast(F32), ALU.subtract)\
                    .then_inc(split_done, 1)

            def first(name, j, i=0):
                ve.wait_ge(tile_done, 2 * i + (F0[name] + j + 1))
                return bank(T0[name] + 2 * j)

            def second(name, j, i=0):
                ve.wait_ge(panel_done, 2 * i + (N0[name] + j + 1))
                return bank(T0[name] + 2 * j + 1)

            def scaled(dst, src, parts=slice(0, P)):
                ve.tensor_tensor(dst, src[parts, :], rstd[parts, :], ALU.mult).then_inc(bank_free, 1)

            def add_square(q, k, kk=None):
                ve.wait_ge(sem("sq_ready"), k + (8 * q + 1))
                if q or k:
                    ve.wait_ge(sem("sq_added"), k + 8 * q)
                ve.tensor_tensor(sqacc[:, :], sqacc[:, :], sq[:, (k if kk is None else kk) % 2], ALU.add)\
                    .then_inc(sem("sq_added"), 1)

            def gain(q, k):
                return par[:, bass.ds(NORMS[q] + k, 1)]

            def low(dst, src, high, wait, count, sig, scale=None):
                ve.wait_ge(sem(wait), count)
                if scale is None:
                    ve.tensor_tensor(dst, src, high.bitcast(F32), ALU.subtract).then_inc(sem(sig), 1)
                else:
                    ve.scalar_tensor_tensor(out=dst, in0=src, scalar=scale, in1=high.bitcast(F32), op0=ALU.mult,
                                            op1=ALU.subtract).then_inc(sem(sig), 1)

            def low_norm(q, k):
                low(act_lo[:, k], x[:, k], act_hi[:, k], f"xhi{q}", k + 1, f"act{q}", gain(q, k))

            def inv(q):
                ve.wait_ge(sem("std_ready"), q + 1)
                ve.memset(sqacc[:, :], 0.0)
                seq.link(ve.reciprocal(rstd[:, :], rstd[:, :]))

            def inv_tokens(q, count):
                ve.wait_ge(sem("std_ready"), q + 1)
                ve.reciprocal(tok_rstd, tok_rstd).then_inc(sem("tok_inv"), 1)
                if q != OUT:
                    ve.memset(sqacc[:, :], 0.0)
                if q == FINAL:
                    lo(N0["glr"] + 1)
                ve.wait_ge(sem("rstd_repeated"), count)

            ve.memset(prow[:, :, :], 0.0).then_inc(sem("prow_zero"), 1)
            ve.memset(eps6[:, :], 1e-6)
            ve.memset(eps5[:, :], 1e-5).then_inc(sem("consts_set"), 1)
            ve.memset(t1[:, :, :], 0.0).then_inc(bank_free, 4)
            ve.memset(t2[:, :, :], 0.0).then_inc(sem("pv_out"), 1)
            ve.memset(t3[:, :, :], 0.0).then_inc(sem("pv_ready"), 1)
            seq.link(ve.memset(sqacc[:, :], 0.0))

            for k in range(KD):
                ve.wait_ge(sem("setup_ready"), k + 1)
                ve.tensor_copy(x[:, k], ps[4 + k % 4][:, :]).then_inc(sem("setup_copied"), 1)
            ve.wait_ge(sem("setup_ready"), KD + 1)
            ve.tensor_copy(par[:, :], ps[4][:, :]).then_inc(sem("setup_copied"), 1)
            ve.wait_ge(sem("setup_copied"), KD + 1)
            lo(0)
            for k in range(KD):
                low_norm(MIX, k)
                add_square(MIX, k)

            for i in range(2):
                lo(N0["q"] + i + 1)
                if i == 0:
                    inv(MIX)
                for c in range(2):
                    src = (second if c else first)("q", i)
                    ve.scalar_tensor_tensor(out=q_f[:, 2 * i + c], in0=src[:, :], scalar=DH ** -0.5, in1=rstd[:, :],
                                            op0=ALU.mult, op1=ALU.mult).then_inc(bank_free, 1)
                for k in (2 * i, 2 * i + 1):
                    low(q_lo[:, k], q_f[:, k], q_hi[:, k], "q_hi", k + 1, "q_lo")
            lo(N0["kvc"] + 1)
            for j in range(2):
                src = (second if j else first)("kvc", 0)
                scaled(kvc[:, j], src)
            ve.wait_ge(bank_free, T0["kvc"] + 6)

            def spread(j):
                for g in range(GR):
                    for odd in range(2):
                        ins = ve.tensor_copy(c2[odd * DH:(odd + 1) * DH, g, 0:S - odd],
                                             kvc[g * DH:(g + 1) * DH, j, odd:S])
                seq.link(ins)

            def blocks(j):
                pos = par[:, COL["cmp_pos_v" if j else "cmp_pos_k"]:][:, 0:16]
                for g in range(GR):
                    for h in range(2):
                        src = c2[:, g, 16 * h:16 * h + 16 * NCMP].rearrange("p (n l b) -> p l n b", l=8, b=2)[:, :, :, 0]
                        ins = ve.tensor_tensor(cmpf[:, 8 * h:8 * h + 8, g * NCMP:(g + 1) * NCMP], src,
                                               pos[:, 8 * h:8 * h + 8].unsqueeze(2).broadcast_to([P, 8, NCMP]),
                                               ALU.add)
                ins.then_inc(sem("cmp_set"), 1)

            spread(0)
            blocks(0)
            lo(N0["gate"] + 1)
            ve.wait_ge(panel_done, N0["gate"] + 1)
            scaled(t1[0:24, 0], bank(T0["gate"]), slice(0, 24))
            lo(N0["u"] + 1)
            ve.wait_ge(sem("att_zero"), 3)
            ve.wait_ge(sem("q_lo"), 4)
            for c in range(2):
                scaled(up[:, c, PPAD:], (second if c else first)("u", 0))
            ve.wait_ge(sem("gT_ready"), 1)
            seq.link(ve.tensor_copy(g_tm[:, :, :].rearrange("p b c -> p (b c)"), ps[7][:, 0:TB * 24]))
            lo(N0["u"] + 2)
            for c in range(2):
                scaled(up[:, 2 + c, PPAD:], (second if c else first)("u", 1))
            low(cmp_lo[:, :, :], cmpf[:, :, :], cmp_hi[:, :, :], "cmp_hi", 1, "cmp_lo")
            spread(1)
            blocks(1)
            for j, name in enumerate(("ck", "cv")):
                if j:
                    low(cmp_lo[:, :, :], cmpf[:, :, :], cmp_hi[:, :, :], "cmp_hi", 2, "cmp_lo")
                lo(N0[name] + 1)
                ve.wait_ge(panel_done, N0[name] + 1)
                ve.tensor_copy(t1[:, j, 0:62], bank(T0[name])[:, 0:62]).then_inc(bank_free, 1)
            ve.wait_ge(sem("kcmp_ready"), 1)
            for g in range(GR):
                ins = ve.tensor_copy(kbd[g * DH:(g + 1) * DH, g * NCP:g * NCP + NCMP],
                                     ps[4][0:DH, g * NCMP:(g + 1) * NCMP])
            ins.then_inc(sem("kbd_ready"), 1)
            low(kbd_lo[:, :], kbd[:, :], kbd_hi[:, :], "kbd_hi", 1, "kbd_lo")
            ve.wait_ge(sem("vcmp_ready"), 1)
            for g in range(GR):
                for r in range(HPG):
                    ins = ve.tensor_copy(vbd[r * NCP:r * NCP + NCMP, g, r * DH:(r + 1) * DH],
                                         ps[5][0:NCMP, g * DH:(g + 1) * DH])
            ins.then_inc(sem("vbd_ready"), 1)
            lo(N0["kvs"] + 1)
            scaled(k_f[:, 0], first("kvs", 0))
            scaled(vf[:, 0], second("kvs", 0))
            ve.wait_ge(sem("att_consts"), 16 * 7)
            ve.wait_ge(sem("c_scores"), 1)
            cs = s_sb[:, 0, 0:1024]
            for b in range(2):
                ins = ve.tensor_tensor(s_sb[:, 0, b * S:(b + 1) * S], ps[4 + b][:, :],
                                       cbias[:, 2 * b:2 * b + 2, :].rearrange("p b c -> p (b c)"), ALU.add)
            seq.link(ins)
            c3 = cs.rearrange("p (a n) -> p a n", n=NCP)

            def over(v):
                return v.unsqueeze(2).broadcast_to([P, 32, NCP])
            seq.link(ve.tensor_reduce(cmx[:, :], c3, AXX, ALU.max))
            ve.tensor_tensor(c3, c3, over(cmx[:, :]), ALU.subtract).then_inc(sem("c_shifted"), 1)
            low(k_lo[:, 0], k_f[:, 0], k_hi[:, 0], "k_hi", 1, "k_lo")
            ve.wait_ge(sem("c_exp"), 1)
            seq.link(ve.tensor_reduce(csm[:, :], c3, AXX, ALU.add))
            seq.link(ve.reciprocal(csm[:, :], csm[:, :]))
            for b in range(TB):
                ins = ve.tensor_tensor(csm[:, 8 * b:8 * b + 8], csm[:, 8 * b:8 * b + 8],
                                       g_tm[:, b, :].rearrange("p (h n) -> p h n", n=3)[:, :, 0], ALU.mult)
            seq.link(ins)
            seq.link(ve.tensor_tensor(c3, c3, over(csm[:, :]), ALU.mult))
            for b in range(TB):
                pb = s_sb[:, 0, b * 256:(b + 1) * 256].rearrange("p (h n) -> p h n", n=NCP)
                ins = ve.tensor_tensor(pb, pb, cvalid[:, b, :].unsqueeze(1).broadcast_to([P, 8, NCP]), ALU.mult)
            ins.then_inc(sem("c_probs"), 1)
            lo(N0["kvw"] + 1)
            scaled(k_f[:, 1], first("kvw", 0))
            scaled(vf[:, 1], second("kvw", 0))
            low(k_lo[:, 1], k_f[:, 1], k_hi[:, 1], "k_hi", 2, "k_lo")
            ve.wait_ge(sem("c_pT"), 1)
            for g in range(GR):
                ins = ve.tensor_copy(pc_t[:, g], ps[4 + g][:, :])
            ins.then_inc(sem("c_pT_copied"), 1)
            for br in range(2):
                ve.wait_ge(sem("vT_ready"), br + 1)
                seq.link(ve.tensor_copy(v_tm[:, br, :, :].rearrange("p k c -> p (k c)"), ps[6 + br][:, :]))
            for b in (0, 2):
                ve.wait_ge(sem("c_pv"), b + 1)
                ins = ve.tensor_copy(acc[:, b], ps[b][:, :])
            ins.then_inc(sem("c_done"), 1)
            ve.wait_ge(sem("c_done"), 1)
            ve.wait_ge(sem("pt_a"), 1)

            def softmax(u, g):
                ve.wait_ge(sem("s_ready"), u + 1)
                ve.wait_ge(sem("staged"), u + 1)
                ve.memset(nmx[:, g, :], 0.0)
                for qb, bk, c in ((3, 0, 0), (2, 1, 0), (0, 1, 384), (1, 2, 0)):
                    w = (qb + 1) * P
                    ins = ve.tensor_tensor_reduce(s_sb[:, g, OFF[qb]:OFF[qb] + w], ps[3 * g + bk][:, c:c + w],
                                                  biast[:, g, S - w:S], 1.0, -3e38, ALU.add, ALU.max,
                                                  mx[:, g, qb:qb + 1])
                seq.link(ins)
                ve.tensor_scalar(nmx[:, g, :], mx[:, g, :], -1.0, None, ALU.mult).then_inc(sem("nmax_ready"), 1)

            def output(u, r, b, g, then=None):
                ve.wait_ge(sem("p_ready"), u + 1)
                seq.link(ve.reciprocal(rec[:, :], sm[:, g, :]))
                seq.link(ve.tensor_tensor(rg[:, :].unsqueeze(2), rec[:, :].unsqueeze(2),
                                          g_tm[:, :, bass.ds(3 * r + (12 * g + 1 + b), 1)], ALU.mult))
                ve.wait_ge(sem("pt_ready"), 3 * u + 3)
                ve.tensor_copy(pt[:, 512:1024], ps[7][:, :]).then_inc(sem("pt_v"), 1)
                if then:
                    then()
                ve.wait_ge(sem("pv_ready"), u + 2)
                seq.link(ve.tensor_tensor(otmp[:, :, :], ps[7][:, 0:TB * DH].rearrange("p (b d) -> p b d", b=TB),
                                          rg[:, :].unsqueeze(2).broadcast_to([P, TB, DH]), ALU.mult))
                o = acc[:, :, bass.ds(DH * r + g * HPG * DH, DH)]
                ve.tensor_tensor(o, o, otmp[:, :, :], ALU.add).then_inc(sem("pv_out"), 1)
                ve.wait_ge(sem("pv_out"), u + 2)

            def pooled(gi):
                ve.wait_ge(*((sem("pooled"), gi + 1) if gi < 3 else (panel_done, N0["pool"] + 1)))
                ve.tensor_scalar(y_f[gi], ps[6 + gi % 2][:, :],
                                 par[:, COL["pool_scale"] + gi:COL["pool_scale"] + gi + 1], None, ALU.mult)\
                    .then_inc(bank_free, 1)

            for gi in range(4):
                low(act_lo[:, 4 + gi], up[:, gi, PPAD:], act_hi[:, 4 + gi], "d_hi", gi + 1, "d_lo")
            softmax(0, 0)
            pooled(0)
            pooled(1)
            softmax(1, 1)
            pooled(2)
            pooled(3)
            for gi in range(4):
                low(act_lo[:, 4 + gi], y_f[gi], act_hi[:, 4 + gi], "y_hi", gi + 1, "y_lo")
            for b in range(2):
                with ve.Fori(0, HPG - 1) as r:
                    seq.loop(r, 8)
                    for g in range(GR):
                        output(2 * r + (8 * b + g), r, b, g, lambda: softmax(2 * r + (8 * b + g + 2), g))
                    seq.done(HPG - 1)
                for g in range(GR):
                    output(8 * b + 6 + g, HPG - 1, b, g, (lambda: softmax(8 + g, g)) if b == 0 else None)

            lo(N0["pool"] + 1)
            for k in range(4):
                low(act_lo[:, k], ps[4 + k][:, :], act_hi[:, k], "o_hi", k + 1, "o_lo")

            def late(q, name, bias=None):
                for i in range(4):
                    lo(N0[name] + i + 1)
                    for c in range(2):
                        k = 2 * i + c
                        src = (second if c else first)(name, i)
                        if bias is None:
                            ve.tensor_tensor(x[:, k], x[:, k], src[:, :], ALU.add).then_inc(bank_free, 1)
                        else:
                            ve.scalar_tensor_tensor(out=x[:, k], in0=src[:, :], scalar=par[:, bias + k:bias + k + 1],
                                                    in1=x[:, k], op0=ALU.add, op1=ALU.add).then_inc(bank_free, 1)
                        add_square(q, k)
                for k in range(KD):
                    low_norm(q, k)

            late(FFN1, "mix")

            def ffn(f, q, up_, dn, qn):
                inv(q)
                with ve.Fori(0, KF // 2) as i:
                    for j in range(2):
                        lo(N0[up_] + j + 1, i)
                        scaled(t1[:, j], first(up_, j, i))
                        scaled(t2[:, j], second(up_, j, i))
                        ve.wait_ge(sem("silu_ready"), 2 * i + (KF * f + j + 1))
                        ve.wait_ge(bank_free, 4 * i + (T0[up_] + 2 * j + 6))
                        ve.tensor_tensor(t1[:, j], t2[:, j], t3[:, j], ALU.mult).then_inc(sem("hidden_set"), 1)
                        k = bass.ds(2 * i + j, 1)
                        ve.wait_ge(sem("hidden_hi"), 2 * i + (KF * f + j + 1))
                        ve.tensor_tensor(hid_lo[:, k, :], t1[:, j], hid_hi[:, k, :].bitcast(F32), ALU.subtract)\
                            .then_inc(sem("hidden_lo"), 1)
                if qn == FINAL:
                    ve.wait_ge(sem("hidden_lo"), KF * (f + 1))
                with ve.Fori(0, 2) as i:
                    for j in range(4):
                        lo(N0[dn] + 2 * j + 1, 4 * i)
                        lo(N0[dn] + 2 * j + 2, 4 * i)
                        ve.wait_ge(panel_done, 8 * i + (N0[dn] + 2 * j + 2))
                        k = 4 * i + j
                        xk = x[:, bass.ds(k, 1), :]
                        ve.tensor_tensor(xk, xk, bank(T0[dn] + j)[:, :], ALU.add).then_inc(bank_free, 1)
                        add_square(qn, k, j)
                        if qn != FINAL:
                            kk = bass.ds(k, 1)
                            low(act_lo[:, kk, :], xk, act_hi[:, kk, :], f"xhi{qn}", k + 1, f"act{qn}", gain(qn, k))

            ffn(0, FFN1, "up1", "dn1", CONVIN)

            ve.memset(z[:, 0, 0:CPAD], 0.0).then_inc(sem("conv_done"), 2)
            ve.memset(z[:, 1, 0:CPAD], 0.0).then_inc(sem("zc_ready"), 2)
            inv(CONVIN)
            taps_of = par[:, P:P + CONV * KD].rearrange("p (t m) -> p t m", m=KD)

            def combine(m, j):
                ve.wait_ge(sem("conv_done"), m + 3)
                ve.tensor_tensor(zc[:, bass.ds(m, 1), :], t2[:, j].unsqueeze(1), ps[5 + j][:, :].unsqueeze(1), ALU.add)\
                    .then_inc(sem("zc_ready"), 1)

            def convolve(i, j, only=False):
                m = 2 * i + j
                seq.link(ve.tensor_copy(wtap[:, j].unsqueeze(2), taps_of[:, :, bass.ds(m, 1)]))
                scaled(t1[:, j], first("pw1", j, i))
                scaled(t2[:, j], second("pw1", j, i))
                ve.wait_ge(sem("glu_sig"), m + 1)
                ve.scalar_tensor_tensor(out=z[:, j, CPAD:], in0=t1[:, j],
                                        scalar=par[:, bass.ds(2 * i + (COL["conv_b_pw1"] + j), 1)],
                                        in1=t3[:, j], op0=ALU.add, op1=ALU.mult).then_inc(sem("z_ready"), 1)
                ve.wait_ge(sem("z_ready"), m + 1)
                for tap in range(PETAPS, CONV):
                    zt, w, s = z[:, j, tap:tap + S], wtap[:, j, tap:tap + 1], (t2, t1)[(tap - PETAPS) % 2][:, j]
                    if tap == PETAPS:
                        ins = ve.tensor_scalar(s, zt, w, par[:, bass.ds(2 * i + (COL["conv_b_dw"] + j), 1)],
                                               ALU.mult, ALU.add)
                    elif tap == PETAPS + 1:
                        ins = ve.tensor_scalar(s, zt, w, None, ALU.mult)
                    else:
                        ins = ve.scalar_tensor_tensor(out=s, in0=zt, scalar=w, in1=s, op0=ALU.mult, op1=ALU.add)
                    seq.link(ins, behind=int(tap < CONV - 1))
                seq.link(ve.tensor_tensor(t2[:, j], t2[:, j], t1[:, j], ALU.add))
                if not only:
                    combine(m - 1, 1 - j)

            convolve(0, 0, True)
            convolve(0, 1)
            with ve.Fori(1, 4) as i:
                per = 2 * (CONV - PETAPS + 2)
                seq.loop(i, per, 1)
                for j in range(2):
                    convolve(i, j)
                seq.done(3)
            combine(KD - 1, 1)
            ve.wait_ge(sem("zc_ready"), KD + 2)
            ve.wait_ge(sem("zmean_ready"), 1)
            seq.link(ve.tensor_scalar(mean[:, :], ps[7][:, :], 1.0 / D, None, ALU.mult))
            for k in range(KD):
                ve.tensor_tensor(zc[:, k], zc[:, k], mean[:, :], ALU.subtract).then_inc(sem("ln_centered"), 1)
                if k:
                    add_square(LN, k - 1)
            add_square(LN, KD - 1)
            inv_tokens(LN, 1)
            for k in range(KD + 1):
                if k < KD:
                    if k >= 2:
                        ve.wait_ge(sem("zhi"), k - 1)
                    ve.wait_ge(sem("ln_centered"), k + 1)
                    ve.tensor_tensor(t1[:, k % 2], zc[:, k], ps[5][:, :], ALU.mult).then_inc(sem("ln_scaled"), 1)
                if k:
                    low(act_lo[:, k - 1], t3[:, (k - 1) % 2], act_hi[:, k - 1], "zhi", k, "zlo")
            ve.wait_ge(split_done, N0["pw2"] + 1)
            late(FFN2, "pw2", COL["conv_b_pw2"])
            ffn(1, FFN2, "up2", "dn2", FINAL)

            inv_tokens(FINAL, 2)
            for k in range(KD):
                ve.scalar_tensor_tensor(out=x[:, k], in0=x[:, k], scalar=gain(FINAL, k), in1=ps[5][:, :],
                                        op0=ALU.mult, op1=ALU.mult).then_inc(sem("x_final"), 1)
                if k:
                    add_square(GLAIN, k - 1)
                    low_norm(GLAIN, k - 1)
            add_square(GLAIN, KD - 1)
            low_norm(GLAIN, KD - 1)

            inv_tokens(GLAIN, 3)
            seq.link(ve.tensor_copy(rstd[:, :], ps[5][:, :]))
            ve.wait_ge(panel_done, N0["glr"] + 1)
            scaled(glr[:, :], bank(T0["glr"]), slice(0, 16))
            for i, dst in enumerate((q2, k2)):
                lo(N0["qk2"] + i + 1)
                if i:
                    for c in range(2):
                        ve.wait_ge(sem("logit_mm"), c + 1)
                        ve.tensor_scalar(la[:, c * S:(c + 1) * S], ps[4 + c][:, :],
                                         par[:, COL["b_gate_2"] + c:COL["b_gate_2"] + c + 1], None, ALU.add)\
                            .then_inc(sem("logit_ready"), 1)
                for c in range(2):
                    src = (second if c else first)("qk2", i)
                    ve.scalar_tensor_tensor(out=dst[:, c], in0=src[:, :], scalar=1.0 if i else GDK ** -0.5,
                                            in1=rstd[:, :], op0=ALU.mult, op1=ALU.mult).then_inc(bank_free, 1)
            lo(N0["v2"] + 1)
            scaled(v2f[:, 0], first("v2", 0))
            ve.wait_ge(sem("gla_set"), 3)
            ve.wait_ge(sem("softplus_ready"), 1)
            seq.link(ve.scalar_tensor_tensor(out=la[:, :], in0=la[:, :], scalar=0.0, in1=la2[:, :], op0=ALU.min,
                                             op1=ALU.subtract))
            seq.link(ve.tensor_tensor_scan(bc[:, :], scan1[:, :], la[:, :], 0.0, ALU.mult, ALU.add))
            ve.tensor_scalar(bc[:, :], bc[:, :], 1.0 / 16.0, None, ALU.mult).then_inc(sem("bc_ready"), 1)
            scaled(v2f[:, 1], second("v2", 0))

            q2f, k2f = (v[:, :, :].rearrange("p c t -> p (c t)") for v in (q2, k2))

            def operands(lev):
                ve.wait_ge(sem("ex_ready"), lev + 1)
                if lev:
                    ve.wait_ge(sem("lev_scores"), 2 * lev)
                ve.tensor_tensor(qd[:, :], q2f, ex[:, :], ALU.mult)
                ve.tensor_tensor(kd[:, :], k2f, ex[:, :], ALU.mult).then_inc(sem("kd_ready"), 1)

            def add_level(lev):
                m = LEVELS[lev]
                for h in range(2):
                    ve.wait_ge(sem("lev_scores"), 2 * lev + h + 1)
                    tmp = t1[:, h, :]
                    seq.link(ve.tensor_tensor(tmp.rearrange("p (a c) -> p a c", c=CH),
                                              ps[6 + h][:, :].rearrange("p (a c) -> p a c", c=CH),
                                              glm[:, lev, :].unsqueeze(1).broadcast_to([P, 2 * TB, CH]), ALU.mult))
                    dst = at[:, 2 * h:2 * h + 2].rearrange("p a t -> p (a t)").rearrange(
                        "p (b t) -> p b t", t=2 * m)[:, :, m:]
                    ve.tensor_tensor(dst, dst, tmp.rearrange("p (b t) -> p b t", t=m), ALU.add)\
                        .then_inc(sem("lev_added"), 1)
                    ve.wait_ge(sem("lev_added"), 2 * lev + h + 1)

            def add_self(half):
                for c in range(2):
                    ve.wait_ge(sem("self_scores"), 2 * half + c + 1)
                    tmp, dst = t1[:, c, :], at[:, 2 * half + c]
                    seq.link(ve.tensor_tensor(tmp.rearrange("p (w t) -> p w t", w=TB),
                                              ps[4 + c][:, :].rearrange("p (w t) -> p w t", w=TB),
                                              ident[:, :].unsqueeze(1).broadcast_to([P, TB, P]), ALU.mult))
                    ve.tensor_tensor(dst, dst, tmp, ALU.add).then_inc(sem("self_added"), 1)
                    ve.wait_ge(sem("self_added"), 2 * half + c + 1)

            def copy_values(half):
                for w in (2 * half, 2 * half + 1):
                    ve.wait_ge(sem("v2T_ready"), w + 1)
                    ve.tensor_copy(v2[:, w], ps[4 + w % 2][:, :]).then_inc(sem("v2_copied"), 1)

            def set_state(ch):
                ve.wait_ge(sem("update_ready"), ch + 1)
                if ch:
                    ve.wait_ge(sem("state_set"), ch)
                for h in range(2):
                    for c in range(2):
                        part = slice(h * GDK, (h + 1) * GDK)
                        up_ps = ps[4 + ch % 4][part, c * 256 + h * GDV:c * 256 + (h + 1) * GDV]
                        e = c * S + ch * CH + CH - 1
                        if ch == 0:
                            ins = ve.tensor_copy(state[part, c, 1, :], up_ps)
                        else:
                            ins = ve.scalar_tensor_tensor(out=state[part, c, ch + 1, :], in0=state[part, c, ch, :],
                                                          scalar=la2[part, e:e + 1], in1=up_ps, op0=ALU.mult,
                                                          op1=ALU.add)
                ins.then_inc(sem("state_set"), 1)

            lo(N0["v2"] + 2)
            scaled(v2f[:, 2], first("v2", 1))
            operands(0)
            scaled(v2f[:, 3], second("v2", 1))
            ve.wait_ge(sem("at_zero"), 1)
            for i in range(2):
                if i:
                    copy_values(0)
                add_level(i)
                lo(N0["cb2"] + i + 1)
                scaled(cbt[:, 2 * i], first("cb2", i))
                operands(1 + i)
                scaled(cbt[:, 2 * i + 1], second("cb2", i))
            copy_values(1)
            for i in range(4):
                if i in (1, 2):
                    add_self(i - 1)
                add_level(2 + i)
                lo(N0["ccx"] + i + 1)
                scaled(t2[:, 0], first("ccx", i))
                if i < 3:
                    operands(3 + i)
                else:
                    ve.wait_ge(sem("ex_ready"), len(LEVELS) + 1)
                    ve.tensor_tensor(kd[:, :], k2f, ex[:, :], ALU.mult).then_inc(sem("kd_ready"), 1)
                    ve.wait_ge(sem("ebc_ready"), 1)
                    seq.link(ve.tensor_tensor(qe[:, :], q2f, la2[:, :], ALU.mult))
                scaled(t2[:, 1], second("ccx", i))
                ve.wait_ge(bank_free, T0["ccx"] + 2 * i + 6)
                if i >= 2:
                    ve.wait_ge(sem("yc_ready"), i - 1)
                ve.tensor_tensor(ccx[:, i % 2, 2:], t2[:, 0], t2[:, 1], ALU.mult).then_inc(sem("ccx_ready"), 1)
            for c in range(2):
                ve.wait_ge(sem("kdT_ready"), c + 1)
                ve.tensor_copy(kdt[:, :, c, :], ps[4 + c][:, :].rearrange("p (w n) -> p w n", w=TB))\
                    .then_inc(sem("kdt_copied"), 1)
            lo(N0["g2"] + 1)
            scaled(gs[:, 0], first("g2", 0))
            for ch in range(4):
                set_state(ch)
            scaled(gs[:, 1], second("g2", 0))
            for ch in range(4, NCH - 1):
                set_state(ch)
            lo(N0["g2"] + 2)
            scaled(gs[:, 2], first("g2", 1))
            for h in range(GH):
                ve.wait_ge(sem("go_ready"), h + 1)
                ve.tensor_copy(gla_o[:, h], ps[4 + h][:, :]).then_inc(sem("go_copied"), 1)
            scaled(gs[:, 3], second("g2", 1))
            ve.wait_ge(sem("go_std"), 1)
            ve.reciprocal(head_rstd[:, :], head_rstd[:, :]).then_inc(sem("go_rstd"), 1)
            for k in range(4):
                low(act_lo[:, 4 + k], cbt[:, k], act_hi[:, 4 + k], "yc_hi", k + 1, "yc_lo")
            for h in range(GH):
                ve.wait_ge(sem("go_scale"), h + 1)
                seq.link(ve.tensor_tensor(gla_o[:, h], gla_o[:, h], ps[4 + (h + 1) % 4][:, :], ALU.mult))
                ve.wait_ge(sem("gs_ready"), h + 1)
                if h >= 2:
                    ve.wait_ge(sem("go_hi"), h - 1)
                ve.scalar_tensor_tensor(out=t1[:, h % 2], in0=gla_o[:, h],
                                        scalar=par[:, COL["gn_g_2"]:COL["gn_g_2"] + 1],
                                        in1=gs[:, h], op0=ALU.mult, op1=ALU.mult).then_inc(sem("go_out"), 1)
                if h:
                    low(act_lo[:, h - 1], t1[:, (h - 1) % 2], act_hi[:, h - 1], "go_hi", h, "go_lo")
            low(act_lo[:, GH - 1], t1[:, (GH - 1) % 2], act_hi[:, GH - 1], "go_hi", GH, "go_lo")
            late(FFN3, "mix2")
            ffn(2, FFN3, "up3", "dn3", PLE)

            inv(PLE)
            for c in range(2):
                low(pf_lo[:, c], ps[5 + c][:, :], pf_hi[:, c], "pf_hi", c + 1, "pf_done")

            def ple(i, j, more):
                if more:
                    lo(N0["ple"] + j + 1, i)
                scaled(t1[:, j], first("ple", j, i))
                src = second("ple", j, i)
                ve.wait_ge(sem("ple_sig"), 2 * i + (j + 1))
                ve.tensor_tensor(t2[:, j], src[:, :], t3[:, j], ALU.mult).then_inc(bank_free, 1)
                ve.wait_ge(bank_free, 4 * i + (T0["ple"] + 2 * j + 6))
                xk = x[:, bass.ds(2 * i + j, 1), :]
                ve.tensor_tensor(xk, xk, t2[:, j], ALU.add).then_inc(sem("ple_x"), 1)
                add_square(OUT, 2 * i + j, j)

            with ve.Fori(0, 3) as i:
                for j in range(2):
                    ple(i, j, True)
            ple(3, 0, True)
            ple(3, 1, False)
            inv_tokens(OUT, 4)
            for k in range(KD):
                ve.scalar_tensor_tensor(out=x[:, k], in0=x[:, k], scalar=gain(OUT, k), in1=ps[5][:, :],
                                        op0=ALU.mult, op1=ALU.mult).then_inc(sem("y_ready"), 1)
            for b in range(TB):
                for c in range(2):
                    ve.wait_ge(sem("yT_ready"), 2 * b + c + 1)
                    ve.tensor_copy(yt[:, b, c * S:(c + 1) * S], ps[(2 * b + c) % 4][:, :]).then_inc(sem("y_copied"), 1)


_CONSTS = ["ident", "dist", "slopes", "cbias", "cvalid", "pinv", "glm"]
_INS = ["x", "mix_norm", "ffn_norm", "nsa_w_in", "cmp_pos_k", "cmp_pos_v", "cmp_k_w1", "cmp_k_w2", "cmp_v_w1",
        "cmp_v_w2", "pool_w", "pool_scale", "mix_w_out", "conv_w_pw1", "conv_b_pw1", "conv_w_dw", "conv_b_dw",
        "conv_ln_g", "conv_ln_b", "conv_w_pw2", "conv_b_pw2", "ffn_w_gate", "ffn_w_up", "ffn_w_down", "final_norm",
        "p_2", "ln1_g_2", "w_in_2", "w_gate_up_2", "b_gate_2", "conv_w_2", "gn_g_2", "w_out_2", "ln2_g_2",
        "w_gate_upffn_2", "w_down_2", "ln3_g_2", "w_ple_gate_2", "w_ple_proj_2", "lnf_g_2"]


def constants():
    import numpy as np
    f = np.float32
    p, c = np.arange(P)[:, None], np.arange(S)[None, :]
    d = p - c + (S - P)
    slope = 2.0 ** (-8.0 * np.arange(1, NH + 1) / NH)
    tok = np.arange(P)[:, None, None] + P * np.arange(TB)[None, :, None]
    end = np.arange(NCP)[None, None, :] * 16 + 31
    cd = tok - end
    valid = (cd >= 0) & (np.arange(NCP)[None, None, :] < NCMP)
    cb = np.where(valid[:, :, None, :], -slope[None, None, :, None] * cd[:, :, None, :], -1e30)
    glm = np.zeros((P, len(LEVELS), CH), f)
    for lev, m in enumerate(LEVELS):
        t = np.arange(CH)
        blk = t // m
        glm[:, lev] = (np.arange(P)[:, None] // m == 2 * blk[None, :])
    return {
        "ident": np.eye(P, dtype=f),
        "dist": np.where(d >= 0, d, 1e30).astype(f),
        "slopes": np.broadcast_to(-slope, (P, NH)).astype(f),
        "cbias": cb.reshape(P, TB, 256).astype(f),
        "cvalid": valid.astype(f),
        "pinv": np.broadcast_to(1.0 / np.arange(1, PPAD + 1), (P, PPAD)).astype(f),
        "glm": glm,
    }


def kernel(**inputs):
    import numpy as _np
    import concourse.bacc as _bacc
    from concourse.bass_utils import run_bass_kernel_spmd as _run

    nc = _bacc.Bacc("TRN2", target_bir_lowering=False, num_devices=1)
    arrays, tensors = {}, {}
    consts = constants()
    for name in _INS + _CONSTS:
        a = _np.ascontiguousarray(consts[name] if name in consts else inputs[name])
        arrays[f"in_{name}_dram"] = a
        tensors[name] = nc.dram_tensor(f"in_{name}_dram", a.shape, mybir.dt.from_np(a.dtype), kind="ExternalInput").ap()
    tensors["out"] = nc.dram_tensor("out_0_dram", (1, S, D), F32, kind="ExternalOutput").ap()
    program(nc, tensors)
    r = _run(nc, [arrays], core_ids=[0])
    return r.results[0]["out_0_dram"]
```
